# Optimizing a Trainium2 kernel written in Bass

```python
import math
import jax, jax.numpy as jnp
from jax import lax
import numpy as np

D_MODEL = 1024
BATCH = 1
SEQ = 256
DEPTH = 1

D_MIX = D_MODEL
ATT_HEADS = 8
HEAD_DIM = 64
D_ATT = ATT_HEADS * HEAD_DIM
CONV_GROUPS = 8
D_CONV = D_MIX - D_ATT
CONV_WIDTH = 31
Q_BLOCK = 128
N_EXPERTS = 32
TOP_K = 4
D_FF = 1024
SWIGLU_LIMIT = 7.0
SWIGLU_ALPHA = 1.702
RMS_EPS = 1e-6
LN_EPS = 1e-5
MASK_VALUE = -1e30
D_IN = 3 * D_ATT + ATT_HEADS + 2 * D_CONV

kernel_name = "hybrid_fox_conformer_moe_layer"

def rmsnorm(x, g):
    xf = x.astype(jnp.float32)
    y = xf * lax.rsqrt(jnp.mean(xf * xf, axis=-1, keepdims=True) + RMS_EPS)
    return (y * g.astype(jnp.float32)).astype(x.dtype)

def layernorm(x, g, b):
    xf = x.astype(jnp.float32)
    mu = jnp.mean(xf, axis=-1, keepdims=True)
    var = jnp.mean(jnp.square(xf - mu), axis=-1, keepdims=True)
    y = (xf - mu) * lax.rsqrt(var + LN_EPS)
    return (y * g.astype(jnp.float32) + b.astype(jnp.float32)).astype(x.dtype)

def forgetting_attention(q, k, v, log_f):
    B, H, T, Dh = q.shape
    scale = 1.0 / math.sqrt(Dh)
    c = lax.cumsum(log_f, axis=2)
    k_pos = jnp.arange(T)
    n_blocks = T // Q_BLOCK

    def one_block(i):
        start = i * Q_BLOCK
        q_blk = lax.dynamic_slice_in_dim(q, start, Q_BLOCK, axis=2)
        c_blk = lax.dynamic_slice_in_dim(c, start, Q_BLOCK, axis=2)
        s = jnp.einsum('bhqd,bhkd->bhqk', q_blk, k).astype(jnp.float32) * scale
        s = s + c_blk[..., :, None] - c[..., None, :]
        q_pos = start + jnp.arange(Q_BLOCK)
        causal = k_pos[None, :] <= q_pos[:, None]
        s = jnp.where(causal, s, MASK_VALUE)
        p = jax.nn.softmax(s, axis=-1).astype(v.dtype)
        return jnp.einsum('bhqk,bhkd->bhqd', p, v)

    o = lax.map(one_block, jnp.arange(n_blocks))
    o = jnp.transpose(o, (1, 0, 3, 2, 4))
    return o.reshape(B, T, H * Dh)

def conformer_conv(glu_in, w_dw, b_dw, ln_g, ln_b):
    a, g = jnp.split(glu_in, 2, axis=-1)
    u = a * jax.nn.sigmoid(g)
    y = lax.conv_general_dilated(
        u, w_dw[:, None, :], window_strides=(1,),
        padding=[(CONV_WIDTH - 1, 0)],
        dimension_numbers=('NWC', 'WIO', 'NWC'),
        feature_group_count=D_CONV) + b_dw
    y = layernorm(y, ln_g, ln_b)
    return jax.nn.silu(y)

def moe_ffn(x, w_router, b_router, w_gu, b_gu, w_down, b_down):
    logits = (x @ w_router + b_router).astype(jnp.float32)
    top_vals, top_idx = lax.top_k(logits, TOP_K)
    top_w = jax.nn.softmax(top_vals, axis=-1)
    gates = jnp.sum(jax.nn.one_hot(top_idx, N_EXPERTS, dtype=jnp.float32)
                    * top_w[..., None], axis=1).astype(x.dtype)

    def expert(acc, params):
        wgu_e, bgu_e, wd_e, bd_e, gate_e = params
        h = x @ wgu_e + bgu_e
        hg, hu = h[:, :D_FF], h[:, D_FF:]
        hg = jnp.minimum(hg, SWIGLU_LIMIT)
        hu = jnp.clip(hu, -SWIGLU_LIMIT, SWIGLU_LIMIT)
        act = (hu + 1.0) * (hg * jax.nn.sigmoid(SWIGLU_ALPHA * hg))
        y = act @ wd_e + bd_e
        return acc + gate_e[:, None] * y, None

    acc0 = jnp.zeros_like(x)
    out, _ = lax.scan(expert, acc0, (w_gu, b_gu, w_down, b_down, gates.T))
    return out

def setup_inputs(seed: int = 0) -> dict:
    key = jax.random.key(seed)
    ks = jax.random.split(key, 20)
    f32 = jnp.float32
    nrm = lambda k, shape, s: jax.random.normal(k, shape, f32) * s
    return {
        "x": nrm(ks[0], (BATCH, SEQ, D_MODEL), 1.0),
        "norm_mix_g": 1.0 + nrm(ks[1], (D_MODEL,), 0.02),
        "w_in": nrm(ks[2], (D_MODEL, D_IN), D_MODEL ** -0.5),
        "b_f": jax.random.uniform(ks[3], (ATT_HEADS,), f32, 1.0, 5.0),
        "b_glu": nrm(ks[4], (2 * D_CONV,), 0.02),
        "w_dw": nrm(ks[5], (CONV_WIDTH, D_CONV), CONV_WIDTH ** -0.5),
        "b_dw": nrm(ks[6], (D_CONV,), 0.02),
        "ln_g": 1.0 + nrm(ks[7], (D_CONV,), 0.02),
        "ln_b": nrm(ks[8], (D_CONV,), 0.02),
        "w_out": nrm(ks[9], (D_MIX, D_MODEL), D_MIX ** -0.5),
        "norm_ffn_g": 1.0 + nrm(ks[10], (D_MODEL,), 0.02),
        "w_router": nrm(ks[11], (D_MODEL, N_EXPERTS), D_MODEL ** -0.5),
        "b_router": nrm(ks[12], (N_EXPERTS,), 0.01),
        "w_gu": nrm(ks[13], (N_EXPERTS, D_MODEL, 2 * D_FF), D_MODEL ** -0.5),
        "b_gu": nrm(ks[14], (N_EXPERTS, 2 * D_FF), 0.02),
        "w_down": nrm(ks[15], (N_EXPERTS, D_FF, D_MODEL), D_FF ** -0.5),
        "b_down": nrm(ks[16], (N_EXPERTS, D_MODEL), 0.02),
        "norm_final_g": 1.0 + nrm(ks[17], (D_MODEL,), 0.02),
    }

def reference(x, norm_mix_g, w_in, b_f, b_glu, w_dw, b_dw, ln_g, ln_b, w_out,
              norm_ffn_g, w_router, b_router, w_gu, b_gu, w_down, b_down,
              norm_final_g):
    B, T, D = x.shape
    h = x
    for _ in range(DEPTH):
        xn = rmsnorm(h, norm_mix_g)
        proj = xn @ w_in
        o0 = 0
        q = proj[..., o0:o0 + D_ATT]; o0 += D_ATT
        k = proj[..., o0:o0 + D_ATT]; o0 += D_ATT
        v = proj[..., o0:o0 + D_ATT]; o0 += D_ATT
        f_logit = proj[..., o0:o0 + ATT_HEADS]; o0 += ATT_HEADS
        glu_in = proj[..., o0:o0 + 2 * D_CONV] + b_glu

        heads = lambda t: jnp.transpose(t.reshape(B, T, ATT_HEADS, HEAD_DIM), (0, 2, 1, 3))
        log_f = jax.nn.log_sigmoid((f_logit + b_f).astype(jnp.float32))
        log_f = jnp.transpose(log_f, (0, 2, 1))
        att_o = forgetting_attention(heads(q), heads(k), heads(v), log_f)

        conv_o = conformer_conv(glu_in, w_dw, b_dw, ln_g, ln_b)

        mixed = jnp.concatenate([att_o, conv_o], axis=-1)
        h = h + mixed @ w_out

        hn = rmsnorm(h, norm_ffn_g).reshape(B * T, D)
        h = h + moe_ffn(hn, w_router, b_router, w_gu, b_gu, w_down, b_down).reshape(B, T, D)
    return rmsnorm(h, norm_final_g)


_drawn_inputs = setup_inputs


def setup_inputs(seed=0):
    import zlib

    import numpy as np

    out = dict(_drawn_inputs(seed))
    spreads = {}
    factors = {'b_gu': 5.555, 'b_down': 6.379, 'norm_final_g': 2.869}
    for name, (base, spread) in spreads.items():
        noise = np.random.default_rng([zlib.crc32(name.encode()), seed]).standard_normal(out[name].shape)
        drawn = base * np.exp(spread * noise) if base else spread * noise
        out[name] = __import__('jax').numpy.asarray(drawn.astype(out[name].dtype))
    for name, factor in factors.items():
        out[name] = (out[name] * factor).astype(out[name].dtype)
    return out
```

```python
from contextlib import ExitStack

import concourse.bass as bass
import numpy as np
from concourse import mybir

F32 = mybir.dt.float32
BF16 = mybir.dt.bfloat16
I32 = mybir.dt.int32
U32 = mybir.dt.uint32
ALU = mybir.AluOpType
ACT = mybir.ActivationFunctionType
AX = mybir.AxisListType

P = 128
TOP_K = 4
Q_BLOCK = 128
SWIGLU_LIMIT = 7.0
SWIGLU_ALPHA = 1.702
RMS_EPS = 1e-6
LN_EPS = 1e-5
MASK_VALUE = -1e30

SLOTS = 16
SLOT = 2048
CAP = 64


def hybrid_layer(nc, x, norm_mix_g, w_in, b_f, b_glu, w_dw, b_dw, ln_g, ln_b, w_out, norm_ffn_g,
                 w_router, b_router, w_gu, b_gu, w_down, b_down, norm_final_g, out):
    _, SEQ, D = x.shape
    HEADS = b_f.shape[0]
    D_CONV = b_dw.shape[0]
    D_ATT = D - D_CONV
    DH = D_ATT // HEADS
    TAPS = w_dw.shape[0]
    E = w_router.shape[1]
    D_FF = w_down.shape[1]
    TB = SEQ // P
    KB = D // P
    CB = D_CONV // P
    FB = D_FF // P
    HALF = D // 2
    PAD = TAPS - 1
    SCALE = float(DH) ** -0.5
    assert SEQ == 2 * P == 2 * Q_BLOCK and D == D_FF == 1024 and D_ATT == D_CONV == HALF == 512
    assert DH == 64 and SEQ % CAP == 0 and E <= P

    PIECES = ["glu_a", "glu_g", "q", "k", "v", "out_conv", "out_att"]
    PIECE_COLS = {"q": 0, "k": D_ATT, "v": 2 * D_ATT,
                  "glu_a": 3 * D_ATT + HEADS, "glu_g": 3 * D_ATT + HEADS + D_CONV}
    F_COL = 3 * D_ATT
    FIRST_CHUNK = 2 * len(PIECES)
    UP_CHUNKS, DOWN_CHUNKS = KB, FB // 2
    CHUNKS = UP_CHUNKS + DOWN_CHUNKS
    assert FIRST_CHUNK <= SLOTS

    UNROLL = next(u for u in range(1, E + 1) if u * CHUNKS % SLOTS == 0)
    LOOP_FROM = E % UNROLL
    LOOPS = E // UNROLL
    ROUNDS = UNROLL * CHUNKS // SLOTS

    def slot_of(e, i):
        return (FIRST_CHUNK + CHUNKS * e + i) % SLOTS

    def uses_of(e, i):
        s = slot_of(e, i)
        n = 1 if s < FIRST_CHUNK and s % 2 == 0 else 0
        return n + sum(1 for j in range(FIRST_CHUNK, FIRST_CHUNK + CHUNKS * e + i + 1) if j % SLOTS == s)

    GROUPS = [(0, [0, 1, 2, 3]), (0, [4, 5, 6, 7])] + [(1, [h, h + 1]) for h in range(0, HEADS, 2)]

    with ExitStack() as ctx:
        def sb(name, shape, dt):
            return ctx.enter_context(nc.sbuf_tensor(name, shape, dt))

        def sem(name):
            return ctx.enter_context(nc.semaphore(name))

        ring = sb("ring", [P, SLOTS * SLOT], F32)

        region_a = sb("region_a", [P, 2048], F32)
        region_b = sb("region_b", [P, 2048], F32)
        region_c = sb("region_c", [P, 2048], F32)
        region_d = sb("region_d", [P, 2048], F32)
        region_e = sb("region_e", [P, 3 * 1152], F32)
        region_f = sb("region_f", [P, 2048], F32)

        x_sb = region_a[:, :].rearrange("p (t d) -> p t d", t=TB)
        mixed_t = region_a[:, :].rearrange("p (k t) -> p k t", k=KB)
        xn = region_b[:, :].rearrange("p (t d) -> p t d", t=TB)
        q_aug = region_b[:, :].rearrange("p (h t) -> p h t", h=HEADS)
        xn_t = region_c[:, :].rearrange("p (k t) -> p k t", k=KB)
        hn_t = xn_t
        k_aug = region_d[:, :].rearrange("p (h t) -> p h t", h=HEADS)
        hn = region_d[:, :].rearrange("p (t d) -> p t d", t=TB)
        result = hn
        v_sb = region_e[:, 0:1024].rearrange("p (s n) -> p s n", s=TB)
        u_pad = region_e[:, 1024:1024 + CB * (SEQ + PAD)].rearrange("p (c t) -> p c t", c=CB)
        ln_tmp = region_e[:, 1024:2048].rearrange("p (c t) -> p c t", c=CB)
        conv_y = region_e[:, 2304:2304 + CB * SEQ].rearrange("p (c t) -> p c t", c=CB)
        hn_parts = region_e[:, 0:3072].bitcast(BF16).rearrange("p (s t d) -> p s t d", s=3, t=TB)
        bgu_raw = region_f[:, :].rearrange("p (a n) -> p a n", a=2)
        probs = region_f[:, 0:1024].rearrange("p (b n) -> p b n", b=2)
        probs_t = region_f[:, 1024:2048].rearrange("p (b n) -> p b n", b=2)
        part_rest = region_f[:, :].rearrange("p (t d) -> p t d", t=TB)

        tok_t = region_a[:, 0:512].rearrange("p (k c) -> p k c", k=KB)
        gate_h = region_a[:, 512:1024]
        sig_h = region_a[:, 1024:1536]
        up_h = region_a[:, 1536:2048]
        act_t = region_b[:, 0:512].rearrange("p (j n) -> p j n", j=4)
        y_sb = region_b[:, 512:1024]
        scatter_sb = region_b[:, 1024:1536].rearrange("p (j n) -> p j n", j=4)
        gates_t = region_b[:, 1536:1792]
        bdown_sb = region_a[:, 512:1536]

        gain_row = sb("gain_row", [P, D], F32)
        bgu_parts = sb("bgu_parts", [96, 2, 1024], BF16)
        bias_sel = sb("bias_sel", [96, E // 2, P], BF16)
        ident = sb("ident", [P, P], F32)
        ident_b = sb("ident_b", [P, P], BF16)
        causal = sb("causal", [P, P], BF16)
        upto = sb("upto", [P, P], BF16)
        ones_b = sb("ones_b", [P, P], BF16)
        mean_w = sb("mean_w", [P, P], F32)
        count_i = sb("count_i", [P, SEQ], I32)
        count = sb("count", [P, SEQ], F32)
        expert_no = sb("expert_no", [P, E], F32)
        vec_rows = sb("vec_rows", [28, P], F32)
        dw_rows = sb("dw_rows", [TAPS, D_CONV], F32)
        cols = sb("cols", [P, 28], F32)
        dw_cols = sb("dw_cols", [P, CB, TAPS], F32)
        G_MIX, B_A, B_G, B_DW, LN_G, LN_B = 0, 8, 12, 16, 20, 24
        wf_sb = sb("wf_sb", [P, KB, HEADS], F32)
        bf_col = sb("bf_col", [HEADS, 1], F32)
        wr_sb = sb("wr_sb", [P, KB, E], F32)
        br_col = sb("br_col", [E, 1], F32)
        stat = sb("stat", [P, 16], F32)
        conv_b = sb("conv_b", [P, SEQ], F32)
        ln_s = sb("ln_s", [P, 2, SEQ], F32)
        fg = sb("fg", [HEADS, 6, SEQ], F32)
        amax = sb("amax", [P, len(GROUPS), 4], F32)
        asum = sb("asum", [P, len(GROUPS), 4], F32)
        logits_t = sb("logits_t", [E, SEQ], F32)
        logits = sb("logits", [P, TB, E], F32)
        top8 = sb("top8", [P, TB, 8], F32)
        top8_i = sb("top8_i", [P, TB, 8], U32)
        top_i = sb("top_i", [P, TB, TOP_K], F32)
        top_w = sb("top_w", [P, 3, TB, TOP_K], F32)
        top_s = sb("top_s", [P, 2, TB], F32)
        onehot = sb("onehot", [P, 2, TB, TOP_K, E], F32)
        chosen = sb("chosen", [P, TB, E], F32)
        chosen_b = sb("chosen_b", [P, TB, E], BF16)
        gates = sb("gates", [P, TB, E], F32)
        place = sb("place", [P, TB, E + 1], F32)
        over_f = sb("over_f", [1, 4, E], F32)
        over = sb("over", [1, 2, E], I32)
        over_all = sb("over_all", [1, 1], I32)
        select = sb("select", [P, TB, CAP], BF16)
        weighted = sb("weighted", [P, TB, 3 * CAP], F32)

        resid = ctx.enter_context(nc.psum_tensor("resid", [P, TB, D], F32))
        work = ctx.enter_context(nc.psum_tensor("work", [P, 4, 512], F32))
        GATE_BANK, UP_BANK, TURN_BANK, OUT_BANK = range(4)
        S_BANKS, T_BANK, O_BANK = (2, 1), 0, 3

        x_in = [sem(f"x_in{t}") for t in range(TB)]
        vecs_in, dw_in, wf_in, bf_in = sem("vecs_in"), sem("dw_in"), sem("wf_in"), sem("bf_in")
        bgu_in, router_in, gain_in, final_gain_in = sem("bgu_in"), sem("router_in"), sem("gain_in"), sem("final_gain_in")
        bdown_in, decay_in, result_out = sem("bdown_in"), sem("decay_in"), sem("result_out")
        slot_full = [sem(f"slot_full{s}") for s in range(SLOTS)]
        slots_used = sem("slots_used")
        ident_step, ident_ready, consts_step, consts_ready = sem("ident_step"), sem("ident_ready"), sem("consts_step"), sem("consts_ready")
        count_ready, aug_zeroed, bgu_step, bgu_ready = sem("count_ready"), sem("aug_zeroed"), sem("bgu_step"), sem("bgu_ready")
        pads_ready, moe_zeroed = sem("pads_ready"), sem("moe_zeroed")
        x_squared, x_mean, x_root, x_scale, xn_ready = sem("x_squared"), sem("x_mean"), sem("x_root"), sem("x_scale"), sem("xn_ready")
        vecs_turned, cols_ready, xn_turned, xnt_ready, x_added = sem("vecs_turned"), sem("cols_ready"), sem("xn_turned"), sem("xnt_ready"), sem("x_added")
        proj_done, glu_sig, u_ready, proj_copied = sem("proj_done"), sem("glu_sig"), sem("u_ready"), sem("proj_copied")
        tap_done, fg_step, decay_exp, decay_ready = sem("tap_done"), sem("fg_step"), sem("decay_exp"), sem("decay_ready")
        mean_done, centred, squared, var_done, var_ready, root_ready = sem("mean_done"), sem("centred"), sem("squared"), sem("var_done"), sem("var_ready"), sem("root_ready")
        ln_step, normed, swish_sig, conv_ready = sem("ln_step"), sem("normed"), sem("swish_sig"), sem("conv_ready")
        scores_done, max_step, max_ready, exp_done, sum_step, probs_ready = sem("scores_done"), sem("max_step"), sem("max_ready"), sem("exp_done"), sem("sum_step"), sem("probs_ready")
        probs_turned, probs_t_ready, att_done, att_copied = sem("probs_turned"), sem("probs_t_ready"), sem("att_done"), sem("att_copied")
        conv_added, h_done, h_squared, h_mean, h_root, h_scale, hn_ready = sem("conv_added"), sem("h_done"), sem("h_squared"), sem("h_mean"), sem("h_root"), sem("h_scale"), sem("hn_ready")
        hn_turned, hnt_act, hnt_dve, part_act, part_dve = sem("hn_turned"), sem("hnt_act"), sem("hnt_dve"), sem("part_act"), sem("part_dve")
        logits_done, logits_t_ready, logits_turned = sem("logits_done"), sem("logits_t_ready"), sem("logits_turned")
        top_step, top_diff, top_exp, gates_ready, chosen_ready = sem("top_step"), sem("top_diff"), sem("top_exp"), sem("gates_ready"), sem("chosen_ready")
        places_done, gates_turned, gates_t_ready, place_ready, over_ready = sem("places_done"), sem("gates_turned"), sem("gates_t_ready"), sem("place_ready"), sem("over_ready")
        select_ready, gathered, tok_t_ready = sem("select_ready"), sem("gathered"), sem("tok_t_ready")
        weighted_ready, weighted_turned, scatter_ready = sem("weighted_ready"), sem("weighted_turned"), sem("scatter_ready")
        gate_clamped, up_clamped, sig_ready, glu_ready, act_ready = sem("gate_clamped"), sem("up_clamped"), sem("sig_ready"), sem("glu_ready"), sem("act_ready")
        act_turned, act_t_ready, y_ready, scattered = sem("act_turned"), sem("act_t_ready"), sem("y_ready"), sem("scattered")
        o_squared, o_mean, o_root, o_scale, result_ready = sem("o_squared"), sem("o_mean"), sem("o_root"), sem("o_scale"), sem("result_ready")

        def piece(name):
            s = 2 * PIECES.index(name)
            view = ring[:, s * SLOT:(s + 2) * SLOT]
            return view.rearrange("p (k n) -> p k n", k=4 if name.startswith("out") else KB)

        def chunk(s):
            return ring[:, s * SLOT:(s + 1) * SLOT]

        def experts(eng, one, peel=0):
            first = LOOP_FROM + peel
            for e in range(first):
                one(e, e, 0)
            with eng.Fori(0, LOOPS - peel // UNROLL) as turn:
                for u in range(UNROLL):
                    one(turn * UNROLL + (first + u), first + u, turn)

        def extras(eng, one):
            eng.wait_ge(over_ready, 1)
            total = eng.value_load(over_all[0:1, 0:1], min_val=0, max_val=E)
            with eng.If(total > 0):
                with eng.Fori(0, E) as e:
                    more = eng.value_load(over[0:1, 0, bass.ds(e, 1)], min_val=0, max_val=1)
                    before = eng.value_load(over[0:1, 1, bass.ds(e, 1)], min_val=0, max_val=E)
                    with eng.If(more > 0):
                        with eng.Fori(0, SEQ // CAP - 1) as r:
                            one(e, r + 1, before * (SEQ // CAP - 1) + r)
            return total

        block = ctx.enter_context(nc.Block())

        @block.sync
        def _(sp):
            for t in range(TB):
                sp.dma_start(x_sb[:, t, :], x[0, t * P:(t + 1) * P, :]).then_inc(x_in[t], 16)
            for name in PIECES:
                s = 2 * PIECES.index(name)
                if name.startswith("out"):
                    first = D_ATT if name == "out_conv" else 0
                    src = w_out[first:first + HALF, :].rearrange("(k p) n -> p k n", p=P)
                else:
                    c = PIECE_COLS[name]
                    src = w_in[:, c:c + 512].rearrange("(k p) n -> p k n", p=P)
                sp.dma_start(piece(name), src).then_inc(slot_full[s], 16)

            released = {"glu_a": (proj_done, CB), "glu_g": (proj_done, CB), "q": (proj_done, CB + 3), "k": (proj_done, CB + 5),
                        "v": (proj_done, CB + 7), "out_conv": (conv_added, 1), "out_att": (h_done, TB)}

            def load_chunk(e, i, s):
                if i < UP_CHUNKS:
                    sp.dma_start(chunk(s), w_gu[e, i * P:(i + 1) * P, :]).then_inc(slot_full[s], 16)
                else:
                    j = 2 * (i - UP_CHUNKS)
                    src = w_down[e, j * P:(j + 2) * P, :].rearrange("(b p) n -> p b n", p=P)
                    sp.dma_start(chunk(s).rearrange("p (b n) -> p b n", b=2), src).then_inc(slot_full[s], 16)

            def expert(e, k, turn):
                for i in range(CHUNKS):
                    need = CHUNKS * k + i - SLOTS + 1
                    if need > 0:
                        sp.wait_ge(slots_used, turn * (UNROLL * CHUNKS) + need)
                    elif need + FIRST_CHUNK > 0:
                        held_by = PIECES[(need + FIRST_CHUNK - 1) // 2]
                        sp.wait_ge(*released[held_by])
                    load_chunk(e, i, slot_of(k, i))

            experts(sp, expert, peel=UNROLL)

            def extra(e, r, o):
                sp.wait_ge(slots_used, o * CHUNKS + CHUNKS * E)
                for i in range(CHUNKS):
                    load_chunk(e, i, slot_of(E, i))

            extras(sp, extra)
            for t in range(TB):
                sp.wait_ge(result_ready, t + 1)
                sp.dma_start(out[0, t * P:(t + 1) * P, :], result[:, t, :]).then_inc(result_out, 16)
            sp.wait_ge(result_out, 16 * TB)

        @block.gpsimd
        def _(pool):
            nc.gpsimd.memset(ident[:, :], 0.0).then_inc(ident_step, 1)
            pool.wait_ge(ident_step, 1)
            nc.gpsimd.affine_select(out=ident[:, :], in_=ident[:, :], compare_op=ALU.not_equal, fill=1.0,
                                    base=0, pattern=[[-1, P]], channel_multiplier=1).then_inc(ident_ready, 1)
            nc.gpsimd.memset(u_pad[:, :, 0:PAD], 0.0).then_inc(pads_ready, 1)
            nc.gpsimd.memset(mean_w[:, :], 1.0 / D_CONV).then_inc(consts_ready, 1)
            nc.gpsimd.memset(ones_b[:, :], 1.0).then_inc(consts_ready, 1)
            nc.gpsimd.memset(ident_b[:, :], 0.0).then_inc(consts_step, 1)
            nc.gpsimd.memset(causal[:, :], 0.0).then_inc(consts_step, 1)
            nc.gpsimd.memset(upto[:, :], 1.0).then_inc(consts_step, 1)
            nc.gpsimd.memset(bias_sel[:, :, :], 0.0).then_inc(consts_step, 1)
            pool.wait_ge(consts_step, 4)
            nc.gpsimd.affine_select(out=ident_b[:, :], in_=ident_b[:, :], compare_op=ALU.not_equal, fill=1.0,
                                    base=0, pattern=[[-1, P]], channel_multiplier=1).then_inc(consts_ready, 1)
            nc.gpsimd.affine_select(out=causal[:, :], in_=causal[:, :], compare_op=ALU.is_ge, fill=MASK_VALUE,
                                    base=0, pattern=[[-1, P]], channel_multiplier=1).then_inc(consts_ready, 1)
            nc.gpsimd.affine_select(out=upto[:, :], in_=upto[:, :], compare_op=ALU.is_ge, fill=0.0,
                                    base=0, pattern=[[1, P]], channel_multiplier=-1).then_inc(consts_ready, 1)
            pool.wait_ge(consts_ready, 5)
            pool.wait_ge(xn_turned, 4)
            nc.gpsimd.memset(q_aug[DH:96, :, :], 1.0).then_inc(aug_zeroed, 1)
            pool.wait_ge(aug_zeroed, 1)
            nc.gpsimd.memset(q_aug[96:P, :, :], 0.0).then_inc(aug_zeroed, 1)
            pool.wait_ge(aug_zeroed, 2)
            nc.gpsimd.memset(k_aug[DH:P, :, :], 0.0).then_inc(aug_zeroed, 1)
            pool.wait_ge(aug_zeroed, 3)
            nc.gpsimd.memset(k_aug[DH:DH + 1, :, :], 1.0).then_inc(aug_zeroed, 1)
            pool.wait_ge(aug_zeroed, 4)
            for part in range(3):
                nc.gpsimd.affine_select(
                    out=bias_sel[:, :, :].rearrange("p e (h c) -> p e h c", h=2),
                    in_=bias_sel[:, :, :].rearrange("p e (h c) -> p e h c", h=2),
                    compare_op=ALU.not_equal, fill=1.0, base=-32 * part,
                    pattern=[[-2, E // 2], [-1, 2], [0, CAP]], channel_multiplier=1).then_inc(bgu_step, 1)
                pool.wait_ge(bgu_step, part + 1)
            pool.wait_ge(bgu_in, 16 * 12)
            flat = bgu_parts[:, :, :].rearrange("p g n -> p (g n)")
            raw = region_f[:, :]
            step = 3
            for part in range(3):
                rows = slice(32 * part, 32 * part + 32)
                for again in range(part):
                    nc.gpsimd.tensor_copy(flat[rows, :], raw[rows, :]).then_inc(bgu_step, 1)
                    step += 1
                    pool.wait_ge(bgu_step, step)
                    nc.gpsimd.tensor_tensor(raw[rows, :], raw[rows, :], flat[rows, :], ALU.subtract).then_inc(bgu_step, 1)
                    step += 1
                    pool.wait_ge(bgu_step, step)
                nc.gpsimd.tensor_copy(flat[rows, :], raw[rows, :]).then_inc(bgu_ready, 1)
                pool.wait_ge(bgu_ready, part + 1)
            nc.gpsimd.iota(count_i[:, :], pattern=[[1, SEQ]], base=1, channel_multiplier=0).then_inc(count_ready, 1)
            nc.gpsimd.memset(place[:, :, E:E + 1], 0.0).then_inc(count_ready, 1)
            nc.gpsimd.memset(weighted[:, :, :], 0.0).then_inc(count_ready, 1)
            pool.wait_ge(h_done, TB)
            nc.gpsimd.memset(gates_t[:, :], 0.0).then_inc(moe_zeroed, 1)
            nc.gpsimd.memset(bdown_sb[:, :], 0.0).then_inc(moe_zeroed, 1)

        @block.scalar
        def _(act):
            at = 0
            for vec, n in ((norm_mix_g, KB), (b_glu, 2 * CB), (b_dw, CB), (ln_g, CB), (ln_b, CB)):
                act.dma_start(vec_rows[at:at + n, :], vec.rearrange("(a p) -> a p", p=P)).then_inc(vecs_in, 16)
                at += n
            act.dma_start(dw_rows[:, :], w_dw).then_inc(dw_in, 16)
            act.dma_start(wf_sb[:, :, :], w_in[:, F_COL:F_COL + HEADS].rearrange("(k p) n -> p k n", p=P)).then_inc(wf_in, 16)
            act.dma_start(bf_col[:, :], b_f.rearrange("(a b) -> a b", b=1)).then_inc(bf_in, 16)

            def mean_square(src, junk, into, done):
                nc.scalar.activation(junk, src, ACT.Square, accum_out=into).then_inc(done, 1)

            for t in range(TB):
                act.wait_ge(x_in[t], 16)
                mean_square(x_sb[:, t, :], xn[:, t, :], stat[:, t:t + 1], x_squared)
            for t in range(TB):
                act.wait_ge(x_mean, t + 1)
                nc.scalar.activation(stat[:, 4 + t:5 + t], stat[:, 2 + t:3 + t], ACT.Sqrt).then_inc(x_root, 1)
            for part in range(3):
                for g in range(2):
                    src = b_gu.rearrange("(e g) (u h n) -> g u e h n", g=2, u=2, h=2)[g]
                    for u in range(2):
                        act.dma_start(bgu_raw[32 * part:32 * part + 32, g, u * HALF:(u + 1) * HALF], src[u]).then_inc(bgu_in, 16)
            act.dma_start(wr_sb[:, :, :], w_router.rearrange("(k p) n -> p k n", p=P)).then_inc(router_in, 16)
            act.dma_start(br_col[:, :], b_router.rearrange("(a b) -> a b", b=1)).then_inc(router_in, 16)
            act.dma_start(gain_row[:, :], norm_ffn_g.partition_broadcast(P)).then_inc(gain_in, 16)

            act.wait_ge(cols_ready, 2)
            for c in range(CB):
                act.wait_ge(proj_done, c + 1)
                nc.scalar.activation(conv_y[:, c, :], work[:, c, SEQ:2 * SEQ], ACT.Sigmoid,
                                     bias=cols[:, B_G + c:B_G + c + 1]).then_inc(glu_sig, 1)
            act.wait_ge(proj_done, CB + 1)
            act.wait_ge(bf_in, 16)
            nc.scalar.activation(fg[:, 0, :], work[0:HEADS, 0, 0:SEQ], ACT.Identity, bias=bf_col[:, :]).then_inc(proj_copied, 1)
            for n, (dst, bank) in enumerate(((q_aug, 1), (q_aug, 2), (k_aug, 3), (k_aug, 0))):
                act.wait_ge(proj_done, CB + 2 + n)
                if n == 0:
                    act.wait_ge(xn_turned, 4)
                for odd in range(2):
                    h = 4 * (n % 2) + odd
                    done = nc.scalar.activation(
                        dst[0:DH, h:h + 3:2, :], work[DH * odd:DH * odd + DH, bank, :].rearrange("p (c t) -> p c t", c=2),
                        ACT.Copy)
                done.then_inc(proj_copied, 1)
            act.wait_ge(fg_step, 1)
            nc.scalar.activation(fg[:, 2, :], fg[:, 1, :], ACT.Exp).then_inc(decay_exp, 1)
            act.wait_ge(fg_step, 2)
            nc.scalar.activation(fg[:, 4, :], fg[:, 3, :], ACT.Ln).then_inc(decay_exp, 1)
            act.wait_ge(centred, 1)
            nc.scalar.activation(ln_tmp, conv_y, ACT.Square).then_inc(squared, 1)
            for n in range(TB):
                act.wait_ge(proj_done, CB + 6 + n)
                nc.scalar.activation(v_sb[:, n, :], work[:, (2, 0)[n], :], ACT.Copy).then_inc(proj_copied, 1)
            act.wait_ge(decay_ready, 2)
            act.wait_ge(aug_zeroed, 4)
            act.dma_start(q_aug[DH:DH + 1, :, :], fg[:, 2, :]).then_inc(decay_in, 16)
            act.dma_start(k_aug[DH + 1:DH + 2, :, :], fg[:, 3, :]).then_inc(decay_in, 16)
            act.wait_ge(var_ready, 1)
            nc.scalar.activation(ln_s[:, 1, :], ln_s[:, 0, :], ACT.Sqrt).then_inc(root_ready, 1)
            act.wait_ge(normed, 1)
            for c in range(CB):
                done = nc.scalar.activation(ln_tmp[:, c, :], conv_y[:, c, :], ACT.Sigmoid,
                                            scale=cols[:, LN_G + c:LN_G + c + 1], bias=cols[:, LN_B + c:LN_B + c + 1])
            done.then_inc(swish_sig, 1)

            for g, (_, heads) in enumerate(GROUPS):
                act.wait_ge(max_ready, g + 1)
                if g >= 2:
                    act.wait_ge(probs_turned, g - 1)
                w = 512 // len(heads)
                for n in range(len(heads)):
                    done = nc.scalar.activation(probs[:, g % 2, n * w:(n + 1) * w], work[:, S_BANKS[g % 2], n * w:(n + 1) * w],
                                                ACT.Exp, scale=SCALE, bias=amax[:, g, n:n + 1], accum_out=asum[:, g, n:n + 1])
                done.then_inc(exp_done, 1)
                if g in (3, 5):
                    qb = (g - 3) // 2
                    if qb == 0:
                        act.wait_ge(att_done, 2)
                        nc.scalar.activation(mixed_t[:, 0:4, 0:P], work[:, O_BANK, :].rearrange("p (k t) -> p k t", k=4),
                                             ACT.Copy).then_inc(att_copied, 1)
            act.wait_ge(att_done, len(GROUPS))
            nc.scalar.activation(mixed_t[:, 0:4, P:2 * P], work[:, O_BANK, :].rearrange("p (k t) -> p k t", k=4),
                                 ACT.Copy).then_inc(att_copied, 1)

            for t in range(TB):
                act.wait_ge(h_done, t + 1)
                if t == 0:
                    act.wait_ge(probs_t_ready, len(GROUPS))
                mean_square(resid[:, t, :], hn[:, t, :], stat[:, 8 + t:9 + t], h_squared)
                act.wait_ge(h_mean, t + 1)
                nc.scalar.activation(stat[:, 12 + t:13 + t], stat[:, 10 + t:11 + t], ACT.Sqrt).then_inc(h_root, 1)
            for t in range(TB):
                act.wait_ge(hn_turned, 2 * t + 1)
                nc.scalar.activation(hn_t[:, 0:4, t * P:(t + 1) * P], work[:, 2 * t, :].rearrange("p (k t) -> p k t", k=4),
                                     ACT.Copy).then_inc(hnt_act, 1)
                nc.scalar.activation(hn_parts[:, 0, t, :], hn[:, t, :], ACT.Copy).then_inc(part_act, 1)
            for t in range(TB):
                act.wait_ge(part_dve, t + 1)
                nc.scalar.activation(hn_parts[:, 1, t, :], part_rest[:, t, :], ACT.Copy).then_inc(part_act, 1)
            act.wait_ge(moe_zeroed, 2)
            act.dma_start(bdown_sb[0:E, :], b_down).then_inc(bdown_in, 16)
            act.wait_ge(hn_ready, TB)
            act.dma_start(gain_row[:, :], norm_final_g.partition_broadcast(P)).then_inc(final_gain_in, 16)
            act.wait_ge(logits_done, 1)
            act.wait_ge(router_in, 32)
            nc.scalar.activation(logits_t[:, :], work[0:E, 0, 0:SEQ], ACT.Identity, bias=br_col[:, :]).then_inc(logits_t_ready, 1)
            act.wait_ge(top_diff, 1)
            nc.scalar.activation(top_w[:, 1, :, :], top_w[:, 0, :, :], ACT.Exp).then_inc(top_exp, 1)
            act.wait_ge(gates_turned, 1)
            act.wait_ge(moe_zeroed, 2)
            nc.scalar.activation(gates_t[0:E, :], work[0:E, UP_BANK, 0:SEQ], ACT.Copy).then_inc(gates_t_ready, 1)

            def copy_tokens(g):
                act.wait_ge(gathered, g + 1)
                nc.scalar.activation(region_a[:, 0:512], work[:, OUT_BANK, :], ACT.Copy).then_inc(tok_t_ready, 1)

            def expert_pass(n, g_next):
                act.wait_ge(gate_clamped, n + 1)
                nc.scalar.activation(sig_h, gate_h, ACT.Sigmoid, scale=SWIGLU_ALPHA).then_inc(sig_ready, 1)
                act.wait_ge(weighted_turned, n + 1)
                nc.scalar.activation(region_b[:, 1024:1536], work[:, TURN_BANK, :], ACT.Copy).then_inc(scatter_ready, 1)
                if g_next is not None:
                    copy_tokens(g_next)
                act.wait_ge(slots_used, n * CHUNKS + CHUNKS)
                nc.scalar.activation(y_sb, work[:, OUT_BANK, :], ACT.Copy).then_inc(y_ready, 1)

            copy_tokens(0)
            experts(act, lambda e, k, turn: expert_pass(e, e + 1))

            def extra(e, r, o):
                copy_tokens(o + (E + 1))
                expert_pass(o + E, None)

            total = extras(act, extra)
            act.wait_ge(scattered, total * (SEQ // CAP - 1) + E)
            for t in range(TB):
                mean_square(resid[:, t, :], hn_t[:, 4 * t:4 * t + 4, :].rearrange("p k t -> p (k t)"), stat[:, t:t + 1], o_squared)
            for t in range(TB):
                act.wait_ge(o_mean, t + 1)
                nc.scalar.activation(stat[:, 4 + t:5 + t], stat[:, 2 + t:3 + t], ACT.Sqrt).then_inc(o_root, 1)

        @block.vector
        def _(dve):
            V = nc.vector

            def inv_rms(n, src, mid, into, squared_sem, mean_sem, root_sem, scale_sem):
                dve.wait_ge(squared_sem, n + 1)
                V.tensor_scalar(mid[0], src, 1.0 / D, RMS_EPS, ALU.mult, ALU.add).then_inc(mean_sem, 1)
                dve.wait_ge(root_sem, n + 1)
                V.reciprocal(into, mid[1]).then_inc(scale_sem, 1)
                dve.wait_ge(scale_sem, n + 1)

            for t in range(TB):
                inv_rms(t, stat[:, t:t + 1], (stat[:, 2 + t:3 + t], stat[:, 4 + t:5 + t]), stat[:, 6 + t:7 + t],
                        x_squared, x_mean, x_root, x_scale)
                V.tensor_scalar(xn[:, t, :], x_sb[:, t, :], stat[:, 6 + t:7 + t], None, ALU.mult).then_inc(xn_ready, 1)
            dve.wait_ge(vecs_turned, 1)
            V.tensor_copy(cols[:, :], work[:, 3, 0:28]).then_inc(cols_ready, 1)
            V.tensor_copy(dw_cols[:, :, :], work[:, 3, 32:32 + 32 * CB].rearrange("p (c j) -> p c j", c=CB)[:, :, 0:TAPS])\
                .then_inc(cols_ready, 1)
            dve.wait_ge(cols_ready, 2)
            for n in range(4):
                t, g = n // 2, n % 2
                dve.wait_ge(xn_turned, n + 1)
                V.tensor_tensor(xn_t[:, 4 * g:4 * g + 4, t * P:(t + 1) * P], work[:, n, :].rearrange("p (k t) -> p k t", k=4),
                                cols[:, G_MIX + 4 * g:G_MIX + 4 * g + 4].unsqueeze(2).to_broadcast([P, 4, P]),
                                ALU.mult).then_inc(xnt_ready, 1)

            dve.wait_ge(pads_ready, 1)
            OPS = TAPS + 1
            with dve.Fori(0, CB) as c:
                dve.wait_ge(glu_sig, c + 1)
                V.scalar_tensor_tensor(u_pad[:, c, PAD:PAD + SEQ], work[:, c, 0:SEQ], cols[:, bass.ds(c + B_A, 1)],
                                       conv_y[:, c, :], ALU.add, ALU.mult).then_inc(u_ready, 1)
                dve.wait_ge(u_ready, c + 1)
                for j in range(TAPS):
                    acc = conv_y[:, c, :] if j % 2 == 0 else conv_b[:, :]
                    src, w = u_pad[:, c, j:j + SEQ], dw_cols[:, c, j:j + 1]
                    if j == 0:
                        done = V.tensor_scalar(acc, src, w, cols[:, bass.ds(c + B_DW, 1)], ALU.mult, ALU.add)
                    elif j == 1:
                        done = V.tensor_scalar(acc, src, w, None, ALU.mult)
                    else:
                        dve.wait_ge(tap_done, c * OPS + (j - 1))
                        done = V.scalar_tensor_tensor(acc, src, w, acc, ALU.mult, ALU.add)
                    done.then_inc(tap_done, 1)
                dve.wait_ge(tap_done, c * OPS + TAPS)
                V.tensor_tensor(conv_y[:, c, :], conv_y[:, c, :], conv_b[:, :], ALU.add).then_inc(tap_done, 1)

            dve.wait_ge(proj_copied, 1)
            V.scalar_tensor_tensor(fg[:, 1, :], fg[:, 0, :], -1.0, fg[:, 0, :], ALU.mult, ALU.min).then_inc(fg_step, 1)
            dve.wait_ge(decay_exp, 1)
            V.tensor_scalar(fg[:, 3, :], fg[:, 2, :], 1.0, None, ALU.add).then_inc(fg_step, 1)
            dve.wait_ge(decay_exp, 2)
            V.scalar_tensor_tensor(fg[:, 5, :], fg[:, 0, :], 0.0, fg[:, 4, :], ALU.min, ALU.subtract).then_inc(fg_step, 1)
            V.memset(fg[:, 1, :], 1.0).then_inc(fg_step, 1)
            dve.wait_ge(fg_step, 4)
            V.tensor_tensor_scan(fg[:, 4, :], fg[:, 1, :], fg[:, 5, :], 0.0, ALU.mult, ALU.add).then_inc(fg_step, 1)
            dve.wait_ge(fg_step, 5)
            V.tensor_scalar(fg[:, 2, :], fg[:, 4, :], 1.0 / SCALE, None, ALU.mult).then_inc(decay_ready, 1)
            V.tensor_scalar(fg[:, 3, :], fg[:, 4, :], -1.0 / SCALE, None, ALU.mult).then_inc(decay_ready, 1)

            dve.wait_ge(mean_done, 1)
            V.tensor_tensor(conv_y, conv_y, work[:, 1, 0:SEQ].unsqueeze(1).to_broadcast([P, CB, SEQ]), ALU.subtract)\
                .then_inc(centred, 1)
            dve.wait_ge(var_done, 1)
            V.tensor_scalar(ln_s[:, 0, :], work[:, 3, 0:SEQ], LN_EPS, None, ALU.add).then_inc(var_ready, 1)
            dve.wait_ge(root_ready, 1)
            V.reciprocal(ln_s[:, 0, :], ln_s[:, 1, :]).then_inc(ln_step, 1)
            dve.wait_ge(ln_step, 1)
            V.tensor_tensor(conv_y, conv_y, ln_s[:, 0, :].unsqueeze(1).to_broadcast([P, CB, SEQ]), ALU.mult)\
                .then_inc(normed, 1)
            dve.wait_ge(normed, 1)
            dve.wait_ge(x_added, 1)
            for c in range(CB):
                V.tensor_scalar(mixed_t[:, 4 + c, :], conv_y[:, c, :], cols[:, LN_G + c:LN_G + c + 1],
                                cols[:, LN_B + c:LN_B + c + 1], ALU.mult, ALU.add).then_inc(ln_step, 1)
            dve.wait_ge(ln_step, 1 + CB)
            dve.wait_ge(swish_sig, 1)
            V.tensor_tensor(mixed_t[:, 4:8, :], mixed_t[:, 4:8, :], ln_tmp, ALU.mult).then_inc(conv_ready, 1)

            def row_max(g):
                heads = GROUPS[g][1]
                w = 512 // len(heads)
                dve.wait_ge(scores_done, g + 1)
                V.reduce_max(amax[:, g, 0:len(heads)], work[:, S_BANKS[g % 2], :].rearrange("p (n w) -> p n w", w=w),
                             AX.X).then_inc(max_step, 1)
                dve.wait_ge(max_step, g + 1)
                V.tensor_scalar(amax[:, g, 0:len(heads)], amax[:, g, 0:len(heads)], -SCALE, None, ALU.mult)\
                    .then_inc(max_ready, 1)

            def normalise(g):
                heads = GROUPS[g][1]
                w = 512 // len(heads)
                n = len(heads)
                dve.wait_ge(exp_done, g + 1)
                V.reciprocal(asum[:, g, 0:n], asum[:, g, 0:n]).then_inc(sum_step, 1)
                dve.wait_ge(sum_step, g + 1)
                view = probs[:, g % 2, :].rearrange("p (n w) -> p n w", w=w)
                V.tensor_tensor(view, view, asum[:, g, 0:n].unsqueeze(2).to_broadcast([P, n, w]), ALU.mult)\
                    .then_inc(probs_ready, 1)

            def copy_turned(g):
                dve.wait_ge(probs_turned, g + 1)
                if g >= 2:
                    dve.wait_ge(att_done, g - 1)
                V.tensor_copy(probs_t[:, g % 2, :], work[:, T_BANK, :]).then_inc(probs_t_ready, 1)

            dve.wait_ge(bgu_ready, 3)
            for g in range(len(GROUPS) + 2):
                if g < len(GROUPS):
                    row_max(g)
                if 1 <= g <= len(GROUPS):
                    normalise(g - 1)
                if g >= 2:
                    copy_turned(g - 2)

            dve.wait_ge(gain_in, 16)
            for t in range(TB):
                inv_rms(t, stat[:, 8 + t:9 + t], (stat[:, 10 + t:11 + t], stat[:, 12 + t:13 + t]), stat[:, 14 + t:15 + t],
                        h_squared, h_mean, h_root, h_scale)
                V.scalar_tensor_tensor(hn[:, t, :], resid[:, t, :], stat[:, 14 + t:15 + t], gain_row[:, :],
                                       ALU.mult, ALU.mult).then_inc(hn_ready, 1)
            for t in range(TB):
                dve.wait_ge(hn_turned, 2 * t + 2)
                V.tensor_copy(hn_t[:, 4:8, t * P:(t + 1) * P], work[:, 2 * t + 1, :].rearrange("p (k t) -> p k t", k=4))\
                    .then_inc(hnt_dve, 1)
            for t in range(TB):
                dve.wait_ge(part_act, t + 1)
                V.tensor_tensor(part_rest[:, t, :], hn[:, t, :], hn_parts[:, 0, t, :], ALU.subtract).then_inc(part_dve, 1)
            for t in range(TB):
                dve.wait_ge(part_act, TB + t + 1)
                V.tensor_tensor(hn_parts[:, 2, t, :], part_rest[:, t, :], hn_parts[:, 1, t, :], ALU.subtract).then_inc(part_dve, 1)

            steps = [0]

            def then(ins):
                steps[0] += 1
                ins.then_inc(top_step, 1)
                dve.wait_ge(top_step, steps[0])

            dve.wait_ge(count_ready, 3)
            V.tensor_copy(count[:, :], count_i[:, :]).then_inc(top_step, 1)
            steps[0] += 1
            dve.wait_ge(top_step, 1)
            then(V.tensor_scalar(expert_no[:, :], count[:, 0:E], -1.0, None, ALU.add))
            dve.wait_ge(logits_turned, 1)
            then(V.tensor_copy(logits[:, :, :], work[:, 1, 0:TB * E].rearrange("p (t e) -> p t e", t=TB)))
            for t in range(TB):
                then(V.max(out=top8[:, t, :], in_=logits[:, t, :]))
            for t in range(TB):
                then(V.max_index(out=top8_i[:, t, :], in_max=top8[:, t, :], in_values=logits[:, t, :]))
            V.tensor_tensor(top_w[:, 0, :, :], top8[:, :, 0:TOP_K], top8[:, :, 0:1].to_broadcast([P, TB, TOP_K]),
                            ALU.subtract).then_inc(top_diff, 1)
            then(V.tensor_copy(top_i[:, :, :], top8_i[:, :, 0:TOP_K]))
            for t in range(TB):
                then(V.tensor_tensor(onehot[:, 0, t, :, :], expert_no[:, :].unsqueeze(1).to_broadcast([P, TOP_K, E]),
                                     top_i[:, t, :].unsqueeze(2).to_broadcast([P, TOP_K, E]), ALU.is_equal))
            then(V.tensor_reduce(chosen[:, :, :], onehot[:, 0, :, :, :].rearrange("p t k e -> p t e k"), AX.X, ALU.add))
            V.tensor_copy(chosen_b[:, :, :], chosen[:, :, :]).then_inc(chosen_ready, 1)
            dve.wait_ge(top_exp, 1)
            then(V.reduce_sum(top_s[:, 0, :], top_w[:, 1, :, :], AX.X))
            then(V.reciprocal(top_s[:, 1, :], top_s[:, 0, :]))
            then(V.tensor_tensor(top_w[:, 2, :, :], top_w[:, 1, :, :], top_s[:, 1, :].unsqueeze(2).to_broadcast([P, TB, TOP_K]),
                                 ALU.mult))
            for t in range(TB):
                then(V.tensor_tensor(onehot[:, 1, t, :, :], onehot[:, 0, t, :, :],
                                     top_w[:, 2, t, :].unsqueeze(2).to_broadcast([P, TOP_K, E]), ALU.mult))
            V.tensor_reduce(gates[:, :, :], onehot[:, 1, :, :, :].rearrange("p t k e -> p t e k"), AX.X, ALU.add)\
                .then_inc(gates_ready, 1)
            dve.wait_ge(gates_ready, 1)
            dve.wait_ge(places_done, 1)
            V.tensor_tensor(place[:, :, 0:E], work[:, 2, 0:TB * E].rearrange("p (t e) -> p t e", t=TB), chosen[:, :, :],
                            ALU.mult).then_inc(place_ready, 1)
            dve.wait_ge(place_ready, 1)

            def select_tokens(e, r, g):
                dve.wait_ge(gathered, g)
                for t in range(TB):
                    done = V.tensor_scalar(select[:, t, :], count[:, bass.ds(r * CAP, CAP)], place[:, t, bass.ds(e, 1)], None,
                                           ALU.is_equal)
                done.then_inc(select_ready, 1)

            def weigh_tokens(e, r, g):
                dve.wait_ge(gathered, g + 1)
                for t in range(TB):
                    done = V.tensor_scalar(weighted[:, t, CAP:2 * CAP], count[:, bass.ds(r * CAP, CAP)],
                                           place[:, t, bass.ds(e, 1)], gates[:, t, bass.ds(e, 1)], ALU.is_equal, ALU.mult)
                done.then_inc(weighted_ready, 1)

            def expert_pass(n):
                dve.wait_ge(slots_used, n * CHUNKS + UP_CHUNKS)
                V.tensor_scalar(gate_h, work[:, GATE_BANK, :], SWIGLU_LIMIT, None, ALU.min).then_inc(gate_clamped, 1)
                V.tensor_scalar(up_h, work[:, UP_BANK, :], SWIGLU_LIMIT, -SWIGLU_LIMIT, ALU.min, ALU.max).then_inc(up_clamped, 1)
                dve.wait_ge(gate_clamped, n + 1)
                dve.wait_ge(sig_ready, n + 1)
                V.tensor_tensor(sig_h, sig_h, gate_h, ALU.mult).then_inc(glu_ready, 1)
                dve.wait_ge(glu_ready, n + 1)
                dve.wait_ge(up_clamped, n + 1)
                V.scalar_tensor_tensor(up_h, up_h, 1.0, sig_h, ALU.add, ALU.mult).then_inc(act_ready, 1)
                dve.wait_ge(act_turned, n + 1)
                V.tensor_copy(region_b[:, 0:512], work[:, TURN_BANK, :]).then_inc(act_t_ready, 1)

            select_tokens(0, 0, 0)
            then(V.tensor_scalar(over_f[:, 0, :], work[0:1, 2, TB * E:TB * E + E], float(CAP), None, ALU.is_gt))
            then(V.memset(over_f[:, 3, :], 1.0))
            then(V.tensor_tensor_scan(over_f[:, 1, :], over_f[:, 3, :], over_f[:, 0, :], 0.0, ALU.mult, ALU.add))
            then(V.tensor_tensor(over_f[:, 2, :], over_f[:, 1, :], over_f[:, 0, :], ALU.subtract))
            then(V.tensor_copy(over[:, 0, :], over_f[:, 0, :]))
            then(V.tensor_copy(over[:, 1, :], over_f[:, 2, :]))
            V.tensor_copy(over_all[:, :], over_f[:, 1, E - 1:E]).then_inc(over_ready, 1)

            def expert(e, k, turn):
                weigh_tokens(e, 0, e)
                select_tokens(e + 1, 0, e + 1)
                expert_pass(e)

            experts(dve, expert)

            def extra(e, r, o):
                select_tokens(e, r, o + (E + 1))
                weigh_tokens(e, r, o + (E + 1))
                expert_pass(o + E)

            extras(dve, extra)
            dve.wait_ge(final_gain_in, 16)
            for t in range(TB):
                inv_rms(t, stat[:, t:t + 1], (stat[:, 2 + t:3 + t], stat[:, 4 + t:5 + t]), stat[:, 6 + t:7 + t],
                        o_squared, o_mean, o_root, o_scale)
                V.scalar_tensor_tensor(result[:, t, :], resid[:, t, :], stat[:, 6 + t:7 + t], gain_row[:, :],
                                       ALU.mult, ALU.mult).then_inc(result_ready, 1)

        @block.tensor
        def _(pe):
            def mm(out_, lhsT, rhs, start, stop):
                return nc.tensor.matmul(out_, lhsT, rhs, start=start, stop=stop, skip_group_check=True)

            pe.wait_ge(ident_ready, 1)
            pe.wait_ge(vecs_in, 16 * 5)
            nc.tensor.transpose(work[:, 3, 0:28], vec_rows[:, :], ident[0:28, 0:28])
            pe.wait_ge(dw_in, 16)
            for c in range(CB):
                last = nc.tensor.transpose(work[:, 3, 32 + 32 * c:32 + 32 * c + TAPS], dw_rows[:, c * P:(c + 1) * P],
                                           ident[0:TAPS, 0:TAPS])
            last.then_inc(vecs_turned, 1)
            for n in range(4):
                t, g = n // 2, n % 2
                pe.wait_ge(xn_ready, t + 1)
                if n == 3:
                    pe.wait_ge(cols_ready, 2)
                for j in range(4):
                    last = nc.tensor.transpose(work[:, n, j * P:(j + 1) * P], xn[:, t, (4 * g + j) * P:(4 * g + j + 1) * P], ident[:, :])
                last.then_inc(xn_turned, 1)
            for t in range(TB):
                for h in range(2):
                    last = mm(resid[:, t, h * HALF:(h + 1) * HALF], ident[:, :], x_sb[:, t, h * HALF:(h + 1) * HALF], True, False)
            last.then_inc(x_added, 1)

            def arrived(name):
                pe.wait_ge(slot_full[2 * PIECES.index(name)], 16)

            def columns(bank, at, name, c):
                for kb in range(KB):
                    last = mm(work[:, bank, at:at + SEQ], piece(name)[:, kb, c * P:(c + 1) * P], xn_t[:, kb, :], kb == 0, kb == KB - 1)
                return last

            pe.wait_ge(xnt_ready, 4)
            arrived("glu_a")
            arrived("glu_g")
            for c in range(CB):
                columns(c, 0, "glu_a", c)
                last = columns(c, SEQ, "glu_g", c)
                last.then_inc(proj_done, 1)
            pe.wait_ge(wf_in, 16)
            pe.wait_ge(u_ready, 1)
            for kb in range(KB):
                last = mm(work[0:HEADS, 0, 0:SEQ], wf_sb[:, kb, :], xn_t[:, kb, :], kb == 0, kb == KB - 1)
            last.then_inc(proj_done, 1)
            for n, (name, bank) in enumerate((("q", 1), ("q", 2), ("k", 3), ("k", 0))):
                if n % 2 == 0:
                    arrived(name)
                if n < 3:
                    pe.wait_ge(u_ready, n + 2)
                else:
                    pe.wait_ge(proj_copied, 1)
                columns(bank, 0, name, 2 * (n % 2))
                last = columns(bank, SEQ, name, 2 * (n % 2) + 1)
                last.then_inc(proj_done, 1)

            pe.wait_ge(consts_ready, 5)
            pe.wait_ge(tap_done, CB * (TAPS + 1))
            pe.wait_ge(proj_copied, 2)
            for c in range(CB):
                last = mm(work[:, 1, 0:SEQ], mean_w[:, :], conv_y[:, c, :], c == 0, c == CB - 1)
            last.then_inc(mean_done, 1)
            arrived("v")

            def values(t, bank):
                for kb in range(KB):
                    last = mm(work[:, bank, :], xn_t[:, kb, t * P:(t + 1) * P], piece("v")[:, kb, :], kb == 0, kb == KB - 1)
                last.then_inc(proj_done, 1)

            pe.wait_ge(proj_copied, 3)
            values(0, 2)
            pe.wait_ge(squared, 1)
            pe.wait_ge(proj_copied, 4)
            for c in range(CB):
                last = mm(work[:, 3, 0:SEQ], mean_w[:, :], ln_tmp[:, c, :], c == 0, c == CB - 1)
            last.then_inc(var_done, 1)
            pe.wait_ge(proj_copied, 5)
            values(1, 0)

            def scores(g):
                qb, heads = GROUPS[g]
                bank, w = S_BANKS[g % 2], 512 // len(heads)
                if g >= 2:
                    pe.wait_ge(exp_done, g - 1)
                keys = (qb + 1) * P
                for n, h in enumerate(heads):
                    mm(work[:, bank, n * w:n * w + keys], q_aug[:, h, qb * P:(qb + 1) * P], k_aug[:, h, 0:keys], True, False)
                    last = mm(work[:, bank, n * w + qb * P:n * w + keys], ident_b[:, :], causal[:, :], False, True)
                last.then_inc(scores_done, 1)

            def turn(g):
                pe.wait_ge(probs_ready, g + 1)
                if g >= 1:
                    pe.wait_ge(probs_t_ready, g)
                else:
                    pe.wait_ge(proj_copied, 7)
                for b in range(4):
                    last = nc.tensor.transpose(work[:, T_BANK, b * P:(b + 1) * P], probs[:, g % 2, b * P:(b + 1) * P], ident[:, :])
                last.then_inc(probs_turned, 1)

            def weigh_values(g):
                qb, heads = GROUPS[g]
                pe.wait_ge(probs_t_ready, g + 1)
                if g == 2:
                    pe.wait_ge(att_copied, 1)
                b = 0
                for h in heads:
                    to = work[DH * (h % 2):DH * (h % 2) + DH, O_BANK, (h // 2) * P:(h // 2 + 1) * P]
                    for s in range(qb + 1):
                        last = mm(to, v_sb[:, s, h * DH:(h + 1) * DH], probs_t[:, g % 2, b * P:(b + 1) * P], s == 0, s == qb)
                        b += 1
                last.then_inc(att_done, 1)

            def project(name, t, h):
                for kb in range(4):
                    last = mm(resid[:, t, h * HALF:(h + 1) * HALF],
                              mixed_t[:, (4 if name == "out_conv" else 0) + kb, t * P:(t + 1) * P],
                              piece(name)[:, kb, h * HALF:(h + 1) * HALF], False, False)
                return last

            pe.wait_ge(decay_in, 32)
            pe.wait_ge(proj_copied, 6)
            scores(0)
            pe.wait_ge(centred, 1)
            scores(1)
            pe.wait_ge(conv_ready, 1)
            arrived("out_conv")
            conv_parts = [(t, h) for t in range(TB) for h in range(2)]
            pe.wait_ge(var_ready, 1)
            for g in range(len(GROUPS)):
                turn(g)
                if g + 2 < len(GROUPS):
                    scores(g + 2)
                if conv_parts:
                    last = project("out_conv", *conv_parts.pop(0))
                    if not conv_parts:
                        last.then_inc(conv_added, 1)
                weigh_values(g)
            arrived("out_att")
            for t in range(TB):
                pe.wait_ge(att_copied, t + 1)
                for h in range(2):
                    last = project("out_att", t, h)
                last.then_inc(h_done, 1)
            for t in range(TB):
                pe.wait_ge(hn_ready, t + 1)
                for g in range(2):
                    for j in range(4):
                        last = nc.tensor.transpose(work[:, 2 * t + g, j * P:(j + 1) * P], hn[:, t, (4 * g + j) * P:(4 * g + j + 1) * P], ident[:, :])
                    last.then_inc(hn_turned, 1)
            pe.wait_ge(router_in, 32)
            pe.wait_ge(hnt_act, TB)
            pe.wait_ge(hnt_dve, TB)
            for kb in range(KB):
                last = mm(work[0:E, 0, 0:SEQ], wr_sb[:, kb, :], hn_t[:, kb, :], kb == 0, kb == KB - 1)
            last.then_inc(logits_done, 1)
            pe.wait_ge(logits_t_ready, 1)
            for t in range(TB):
                last = nc.tensor.transpose(work[:, 1, t * E:(t + 1) * E], logits_t[:, t * P:(t + 1) * P], ident[0:E, 0:E])
            last.then_inc(logits_turned, 1)
            pe.wait_ge(chosen_ready, 1)
            for t in range(TB):
                for s in range(t + 1):
                    mm(work[:, 2, t * E:(t + 1) * E], (upto if s == t else ones_b)[:, :], chosen_b[:, s, :], s == 0, s == t)
            for s in range(TB):
                last = mm(work[0:1, 2, TB * E:TB * E + E], ones_b[:, 0:1], chosen_b[:, s, :], s == 0, s == TB - 1)
            last.then_inc(places_done, 1)
            pe.wait_ge(gates_ready, 1)
            for t in range(TB):
                last = nc.tensor.transpose(work[0:E, UP_BANK, t * P:(t + 1) * P], gates[:, t, :], ident[:, :])
            last.then_inc(gates_turned, 1)
            pe.wait_ge(bdown_in, 16)
            pe.wait_ge(gates_t_ready, 1)
            for t in range(TB):
                for h in range(2):
                    mm(resid[:, t, h * HALF:(h + 1) * HALF], gates_t[:, t * P:(t + 1) * P], bdown_sb[:, h * HALF:(h + 1) * HALF], False, False)

            def gather(g):
                pe.wait_ge(select_ready, g + 1)
                for kb in range(KB):
                    for n in range(3 * TB):
                        last = mm(work[:, OUT_BANK, kb * CAP:(kb + 1) * CAP], hn_parts[:, n // TB, n % TB, kb * P:(kb + 1) * P],
                                  select[:, n % TB, :], n == 0, n == 3 * TB - 1)
                last.then_inc(gathered, 1)

            def slot_arrived(k, i, turn):
                pe.wait_ge(slot_full[slot_of(k, i)], turn * (16 * ROUNDS) + 16 * uses_of(k, i))

            def expert_pass(e, n, g, next_g, arrived_chunk, slot):
                pe.wait_ge(tok_t_ready, g + 1)
                for bank in (GATE_BANK, UP_BANK):
                    mm(work[:, bank, :], bias_sel[:, e // 2, :], bgu_parts[:, e % 2, bank * 512:(bank + 1) * 512], True, False)
                for kb in range(KB):
                    arrived_chunk(kb)
                    w = chunk(slot(kb))
                    for bank in (GATE_BANK, UP_BANK):
                        for h in range(2):
                            c = bank * D_FF + h * HALF
                            last = mm(work[CAP * h:CAP * (h + 1), bank, :], tok_t[:, kb, :], w[:, c:c + HALF], False, kb == KB - 1)
                    last.then_inc(slots_used, 1)
                pe.wait_ge(weighted_ready, n + 1)
                for h in range(2):
                    for t in range(TB):
                        last = nc.tensor.transpose(work[:, TURN_BANK, (h * TB + t) * P:(h * TB + t + 1) * P],
                                                   weighted[:, t, (1 - h) * CAP:(1 - h) * CAP + P], ident[:, :])
                last.then_inc(weighted_turned, 1)
                if next_g is not None:
                    gather(next_g)
                pe.wait_ge(act_ready, n + 1)
                pe.wait_ge(scatter_ready, n + 1)
                for j in range(4):
                    last = nc.tensor.transpose(work[:, TURN_BANK, j * P:(j + 1) * P], up_h[:, j * P:(j + 1) * P], ident[:, :])
                last.then_inc(act_turned, 1)
                pe.wait_ge(act_t_ready, n + 1)
                if next_g is not None:
                    pe.wait_ge(tok_t_ready, next_g + 1)
                for m in range(DOWN_CHUNKS):
                    arrived_chunk(UP_CHUNKS + m)
                    w = chunk(slot(UP_CHUNKS + m))
                    for b in range(2):
                        f = 2 * m + b
                        lhsT = act_t[:, f % 4, (f // 4) * CAP:(f // 4 + 1) * CAP]
                        for h in range(2):
                            last = mm(work[CAP * h:CAP * (h + 1), OUT_BANK, :], lhsT, w[:, b * D + h * HALF:b * D + (h + 1) * HALF],
                                      f == 0, f == FB - 1)
                    last.then_inc(slots_used, 1)
                pe.wait_ge(y_ready, n + 1)
                for t in range(TB):
                    for h in range(2):
                        last = mm(resid[:, t, h * HALF:(h + 1) * HALF], scatter_sb[:, h * TB + t, :], y_sb, False, False)
                last.then_inc(scattered, 1)

            gather(0)
            experts(pe, lambda e, k, turn: expert_pass(e, e, e, e + 1, lambda i: slot_arrived(k, i, turn), lambda i: slot_of(k, i)))

            def extra(e, r, o):
                gather(o + (E + 1))
                expert_pass(e, o + E, o + (E + 1), None,
                            lambda i: pe.wait_ge(slot_full[slot_of(E, i)], o * 16 + 16 * uses_of(E, i)), lambda i: slot_of(E, i))

            extras(pe, extra)


_INS = ["x", "norm_mix_g", "w_in", "b_f", "b_glu", "w_dw", "b_dw", "ln_g", "ln_b", "w_out", "norm_ffn_g",
        "w_router", "b_router", "w_gu", "b_gu", "w_down", "b_down", "norm_final_g"]


def kernel(**inputs):
    import concourse.bacc as bacc
    from concourse.bass_utils import run_bass_kernel_spmd

    nc = bacc.Bacc("TRN2", target_bir_lowering=False, num_devices=1, dynamic_dma_scratch_size=1024)
    arrays, args = {}, []
    for name in _INS:
        a = np.ascontiguousarray(inputs[name])
        arrays[f"in_{name}"] = a
        args.append(nc.dram_tensor(f"in_{name}", a.shape, mybir.dt.from_np(a.dtype), kind="ExternalInput").ap())
    result = nc.dram_tensor("result", inputs["x"].shape, F32, kind="ExternalOutput").ap()
    hybrid_layer(nc, *args, result)
    return run_bass_kernel_spmd(nc, [arrays], core_ids=[0]).results[0]["result"]
```

```python
from contextlib import ExitStack

import concourse.bass as bass
import numpy as np
from concourse import mybir

F32 = mybir.dt.float32
BF16 = mybir.dt.bfloat16
I32 = mybir.dt.int32
U32 = mybir.dt.uint32
ALU = mybir.AluOpType
ACT = mybir.ActivationFunctionType
AX = mybir.AxisListType

P = 128
TOP_K = 4
Q_BLOCK = 128
SWIGLU_LIMIT = 7.0
SWIGLU_ALPHA = 1.702
RMS_EPS = 1e-6
LN_EPS = 1e-5
MASK_VALUE = -1e30

SLOTS = 20
SLOT = 2048
CAP = 64


def hybrid_layer(nc, x, norm_mix_g, w_in, b_f, b_glu, w_dw, b_dw, ln_g, ln_b, w_out, norm_ffn_g,
                 w_router, b_router, w_gu, b_gu, w_down, b_down, norm_final_g, out):
    _, SEQ, D = x.shape
    HEADS = b_f.shape[0]
    D_CONV = b_dw.shape[0]
    D_ATT = D - D_CONV
    DH = D_ATT // HEADS
    TAPS = w_dw.shape[0]
    E = w_router.shape[1]
    D_FF = w_down.shape[1]
    TB = SEQ // P
    KB = D // P
    CB = D_CONV // P
    FB = D_FF // P
    HALF = D // 2
    PAD = TAPS - 1
    SCALE = float(DH) ** -0.5
    assert SEQ == 2 * P == 2 * Q_BLOCK and D == D_FF == 1024 and D_ATT == D_CONV == HALF == 512
    assert DH == 64 and SEQ % CAP == 0 and E <= P

    PIECES = ["glu_a", "glu_g", "q", "k", "v", "out_conv", "out_att"]
    PIECE_COLS = {"q": 0, "k": D_ATT, "v": 2 * D_ATT,
                  "glu_a": 3 * D_ATT + HEADS, "glu_g": 3 * D_ATT + HEADS + D_CONV}
    F_COL = 3 * D_ATT
    FIRST_CHUNK = 2 * len(PIECES)
    UP_CHUNKS, DOWN_CHUNKS = KB, FB // 2
    CHUNKS = UP_CHUNKS + DOWN_CHUNKS
    assert FIRST_CHUNK <= SLOTS

    UNROLL = next(u for u in range(1, E + 1) if u * CHUNKS % SLOTS == 0)
    LOOP_FROM = E % UNROLL
    LOOPS = E // UNROLL
    ROUNDS = UNROLL * CHUNKS // SLOTS

    def slot_of(e, i):
        return (FIRST_CHUNK + CHUNKS * e + i) % SLOTS

    def uses_of(e, i):
        s = slot_of(e, i)
        n = 1 if s < FIRST_CHUNK and s % 2 == 0 else 0
        return n + sum(1 for j in range(FIRST_CHUNK, FIRST_CHUNK + CHUNKS * e + i + 1) if j % SLOTS == s)

    GROUPS = [(0, [0, 1, 2, 3]), (0, [4, 5, 6, 7])] + [(1, [h, h + 1]) for h in range(0, HEADS, 2)]

    with ExitStack() as ctx:
        def sb(name, shape, dt):
            return ctx.enter_context(nc.sbuf_tensor(name, shape, dt))

        def sem(name):
            return ctx.enter_context(nc.semaphore(name))

        ring = sb("ring", [P, SLOTS * SLOT], F32)

        region_q = sb("region_q", [P, 2048], F32)
        region_k = sb("region_k", [P, 2048], F32)
        region_x = sb("region_x", [P, 2048], F32)
        T1_PARTS = 2176
        region_m = sb("region_m", [P, T1_PARTS + 2048], F32)

        x_sb = region_q[:, :].rearrange("p (t d) -> p t d", t=TB)
        q_aug = region_q[:, :].rearrange("p (h t) -> p h t", h=HEADS)
        hn = region_q[:, :].rearrange("p (t d) -> p t d", t=TB)
        gate_h, sig_h, up_h = (region_q[:, 512 * n:512 * (n + 1)] for n in range(3))
        result = hn

        xn = region_k[:, :].rearrange("p (t d) -> p t d", t=TB)
        k_aug = region_k[:, :].rearrange("p (h t) -> p h t", h=HEADS)
        h_t = region_k[:, :].rearrange("p (k t) -> p k t", k=KB)
        final_gain, squares = region_k[:, 0:D], region_k[:, D:2 * D]

        xn_t = region_x[:, :].rearrange("p (k t) -> p k t", k=KB)
        probs = region_x[:, 0:1024].rearrange("p (b n) -> p b n", b=2)
        probs_t = region_x[:, 1024:2048].rearrange("p (b n) -> p b n", b=2)
        tok_t = region_x[:, 0:512].rearrange("p (k c) -> p k c", k=KB)
        act_t_flat, y_sb, scatter_flat = (region_x[:, 512 * n:512 * (n + 1)] for n in (1, 2, 3))
        act_t = act_t_flat.rearrange("p (j n) -> p j n", j=4)
        scatter_sb = scatter_flat.rearrange("p (j n) -> p j n", j=4)
        bdown_sb = region_x[:, 512:1536]

        v_sb = region_m[:, 0:1024].rearrange("p (s n) -> p s n", s=TB)
        u_pad = region_m[:, 1024:1024 + CB * (SEQ + PAD)].rearrange("p (c t) -> p c t", c=CB)
        ln_tmp = region_m[:, 1024:2048].rearrange("p (c t) -> p c t", c=CB)
        conv_y = region_m[:, T1_PARTS:T1_PARTS + 1024].rearrange("p (c t) -> p c t", c=CB)
        att_y = region_m[:, T1_PARTS + 1024:T1_PARTS + 2048].rearrange("p (c t) -> p c t", c=CB)
        hn_parts = [region_m[:, at:at + 1536].bitcast(BF16).rearrange("p (s d) -> p s d", s=3) for at in (0, T1_PARTS)]
        gates_t = region_m[:, T1_PARTS + 1536:T1_PARTS + 1536 + SEQ]

        vec_rows = ring[0:36, 17 * SLOT:17 * SLOT + P]
        dw_rows = ring[0:TAPS, 17 * SLOT + P:17 * SLOT + P + D_CONV]
        fg = ring[0:HEADS, 18 * SLOT:18 * SLOT + 6 * SEQ].rearrange("p (n t) -> p n t", n=6)
        count_i = ring[:, 18 * SLOT + 6 * SEQ:18 * SLOT + 7 * SEQ].bitcast(I32)
        bgu_raw = ring[:, 19 * SLOT:20 * SLOT]
        assert SLOTS == 20

        bgu_parts = sb("bgu_parts", [96, 2, 1024], BF16)
        bias_sel = sb("bias_sel", [96, E // 2, P], BF16)
        ident = sb("ident", [P, P], F32)
        ident_b = sb("ident_b", [P, P], BF16)
        causal = sb("causal", [P, P], BF16)
        upto = sb("upto", [P, P], BF16)
        ones_b = sb("ones_b", [P, P], BF16)
        mean_w = sb("mean_w", [P, P], F32)
        count = sb("count", [P, SEQ], F32)
        expert_no = sb("expert_no", [P, E], F32)
        cols = sb("cols", [P, 36], F32)
        dw_cols = sb("dw_cols", [P, CB, TAPS], F32)
        G_MIX, B_A, B_G, B_DW, LN_G, LN_B, G_FFN = 0, 8, 12, 16, 20, 24, 28
        wf_sb = sb("wf_sb", [P, KB, HEADS], F32)
        bf_col = sb("bf_col", [HEADS, 1], F32)
        wr_sb = sb("wr_sb", [P, KB, E], F32)
        br_row = sb("br_row", [P, E], F32)
        stat = sb("stat", [P, 16], F32)
        spare = sb("spare", [P, 3 * SEQ], F32)
        conv_b = spare[:, 0:SEQ]
        ln_s = spare[:, SEQ:3 * SEQ].rearrange("p (n t) -> p n t", n=2)
        logits_t = spare[0:E, 0:SEQ]
        onehot = spare[:, SEQ:SEQ + 2 * TB * TOP_K * E].rearrange("p (n t k e) -> p n t k e", n=2, t=TB, k=TOP_K)
        amax = sb("amax", [P, len(GROUPS), 4], F32)
        asum = sb("asum", [P, len(GROUPS), 4], F32)
        logits = sb("logits", [P, TB, E], F32)
        top8 = sb("top8", [P, TB, 8], F32)
        top8_i = sb("top8_i", [P, TB, 8], U32)
        top_i = sb("top_i", [P, TB, TOP_K], F32)
        top_w = sb("top_w", [P, 3, TB, TOP_K], F32)
        top_s = sb("top_s", [P, 2, TB], F32)
        chosen = sb("chosen", [P, TB, E], F32)
        chosen_b = sb("chosen_b", [P, TB, E], BF16)
        gates = sb("gates", [P, TB, E], F32)
        place = sb("place", [P, TB, E + 1], F32)
        over_f = sb("over_f", [1, 4, E], F32)
        over = sb("over", [1, 2, E], I32)
        over_all = sb("over_all", [1, 1], I32)
        select = sb("select", [P, TB, CAP], BF16)
        weighted = sb("weighted", [P, TB, 3 * CAP], F32)

        resid = ctx.enter_context(nc.psum_tensor("resid", [P, TB, D], F32))
        work = ctx.enter_context(nc.psum_tensor("work", [P, 4, 512], F32))
        GATE_BANK, UP_BANK, TURN_BANK, OUT_BANK = range(4)
        S_BANKS, T_BANK, O_BANK = (1, 2), 3, 0

        x_in = [sem(f"x_in{t}") for t in range(TB)]
        vecs_in, dw_in, wf_in, bf_in = sem("vecs_in"), sem("dw_in"), sem("wf_in"), sem("bf_in")
        bgu_in, router_in, final_gain_in = sem("bgu_in"), sem("router_in"), sem("final_gain_in")
        bdown_in, decay_in, result_out = sem("bdown_in"), sem("decay_in"), sem("result_out")
        slot_full = [sem(f"slot_full{s}") for s in range(SLOTS)]
        slots_used = sem("slots_used")
        ident_step, ident_ready, consts_step, consts_ready = sem("ident_step"), sem("ident_ready"), sem("consts_step"), sem("consts_ready")
        count_step, count_ready, aug_zeroed = sem("count_step"), sem("count_ready"), sem("aug_zeroed")
        bias_sel_ready, bgu_cast, bgu_rest, pads_ready, moe_zeroed = sem("bias_sel_ready"), sem("bgu_cast"), sem("bgu_rest"), sem("pads_ready"), sem("moe_zeroed")
        x_squared, x_mean, x_root, x_scale, xn_ready = sem("x_squared"), sem("x_mean"), sem("x_root"), sem("x_scale"), sem("xn_ready")
        vecs_turned, cols_ready, xn_turned, xnt_ready, x_added = sem("vecs_turned"), sem("cols_ready"), sem("xn_turned"), sem("xnt_ready"), sem("x_added")
        proj_done, proj_copied, u_ready = sem("proj_done"), sem("proj_copied"), sem("u_ready")
        tap_done, fg_step, decay_exp, decay_ready = sem("tap_done"), sem("fg_step"), sem("decay_exp"), sem("decay_ready")
        mean_done, centred, squared, var_done, var_ready, root_ready = sem("mean_done"), sem("centred"), sem("squared"), sem("var_done"), sem("var_ready"), sem("root_ready")
        ln_step, normed, swish_sig, conv_ready = sem("ln_step"), sem("normed"), sem("swish_sig"), sem("conv_ready")
        scores_done, max_step, max_ready, exp_done, sum_step, probs_ready = sem("scores_done"), sem("max_step"), sem("max_ready"), sem("exp_done"), sem("sum_step"), sem("probs_ready")
        probs_turned, probs_t_ready, att_done, att_copied = sem("probs_turned"), sem("probs_t_ready"), sem("att_done"), sem("att_copied")
        conv_added, h_done, h_copied, h_squared, h_mean, h_root, h_scale = sem("conv_added"), sem("h_done"), sem("h_copied"), sem("h_squared"), sem("h_mean"), sem("h_root"), sem("h_scale")
        hn_ready, h_turned, ht_ready, part_act, part_dve = sem("hn_ready"), sem("h_turned"), sem("ht_ready"), sem("part_act"), sem("part_dve")
        logits_done, logits_t_ready, logits_turned = sem("logits_done"), sem("logits_t_ready"), sem("logits_turned")
        top_step, top_diff, top_exp, gates_ready, chosen_ready = sem("top_step"), sem("top_diff"), sem("top_exp"), sem("gates_ready"), sem("chosen_ready")
        places_done, gates_turned, gates_t_ready, place_ready, over_ready = sem("places_done"), sem("gates_turned"), sem("gates_t_ready"), sem("place_ready"), sem("over_ready")
        select_ready, gathered, tok_t_ready = sem("select_ready"), sem("gathered"), sem("tok_t_ready")
        weighted_ready, weighted_turned, scatter_ready = sem("weighted_ready"), sem("weighted_turned"), sem("scatter_ready")
        gate_clamped, up_clamped, sig_ready, glu_ready, act_ready = sem("gate_clamped"), sem("up_clamped"), sem("sig_ready"), sem("glu_ready"), sem("act_ready")
        act_turned, act_t_ready, y_ready, scattered = sem("act_turned"), sem("act_t_ready"), sem("y_ready"), sem("scattered")
        o_squared, o_mean, o_root, o_scale, result_ready = sem("o_squared"), sem("o_mean"), sem("o_root"), sem("o_scale"), sem("result_ready")

        BANK_OF = {n: (n - 1) % 4 for n in range(1, 10)} | {10: 1, 11: 3}
        MEAN_BANK, VAR_BANK = 2, 0

        def piece(name):
            s = 2 * PIECES.index(name)
            view = ring[:, s * SLOT:(s + 2) * SLOT]
            return view.rearrange("p (k n) -> p k n", k=4 if name.startswith("out") else KB)

        def chunk(s):
            return ring[:, s * SLOT:(s + 1) * SLOT]

        def experts(eng, one, peel=0):
            first = LOOP_FROM + peel
            for e in range(first):
                one(e, e, 0)
            with eng.Fori(0, LOOPS - peel // UNROLL) as turn:
                for u in range(UNROLL):
                    one(turn * UNROLL + (first + u), first + u, turn)

        def extras(eng, one):
            eng.wait_ge(over_ready, 1)
            total = eng.value_load(over_all[0:1, 0:1], min_val=0, max_val=E)
            with eng.If(total > 0):
                with eng.Fori(0, E) as e:
                    more = eng.value_load(over[0:1, 0, bass.ds(e, 1)], min_val=0, max_val=1)
                    before = eng.value_load(over[0:1, 1, bass.ds(e, 1)], min_val=0, max_val=E)
                    with eng.If(more > 0):
                        with eng.Fori(0, SEQ // CAP - 1) as r:
                            one(e, r + 1, before * (SEQ // CAP - 1) + r)
            return total

        block = ctx.enter_context(nc.Block())

        @block.sync
        def _(sp):
            for t in range(TB):
                sp.dma_start(x_sb[:, t, :], x[0, t * P:(t + 1) * P, :]).then_inc(x_in[t], 16)
            at = 0
            for vec, n in ((norm_mix_g, KB), (b_glu, 2 * CB), (b_dw, CB), (ln_g, CB), (ln_b, CB), (norm_ffn_g, KB)):
                sp.dma_start(vec_rows[at:at + n, :], vec.rearrange("(a p) -> a p", p=P)).then_inc(vecs_in, 16)
                at += n
            sp.dma_start(dw_rows, w_dw).then_inc(dw_in, 16)
            for name in PIECES:
                s = 2 * PIECES.index(name)
                if name.startswith("out"):
                    first = D_ATT if name == "out_conv" else 0
                    src = w_out[first:first + HALF, :].rearrange("(k p) n -> p k n", p=P)
                else:
                    c = PIECE_COLS[name]
                    src = w_in[:, c:c + 512].rearrange("(k p) n -> p k n", p=P)
                sp.dma_start(piece(name), src).then_inc(slot_full[s], 16)
                if name == "glu_g":
                    src = b_gu.rearrange("(e g) (u h n) -> g u e h n", g=2, u=2, h=2)
                    for part in range(3):
                        for g in range(2):
                            for u in range(2):
                                c = (2 * g + u) * HALF
                                sp.dma_start(bgu_raw[32 * part:32 * part + 32, c:c + HALF], src[g, u]).then_inc(bgu_in, 16)

            released = {"glu_a": (proj_done, 5), "glu_g": (proj_done, 5), "q": (proj_done, 7), "k": (proj_done, 9),
                        "v": (proj_done, 11), "out_conv": (conv_added, 1), "out_att": (h_done, TB)}

            last_use = {17: ((vecs_turned, 1),), 18: ((decay_in, 32), (count_ready, 1)), 19: ((bgu_cast, 4),)}

            def load_chunk(e, i, s):
                if i < UP_CHUNKS:
                    sp.dma_start(chunk(s), w_gu[e, i * P:(i + 1) * P, :]).then_inc(slot_full[s], 16)
                else:
                    j = 2 * (i - UP_CHUNKS)
                    src = w_down[e, j * P:(j + 2) * P, :].rearrange("(b p) n -> p b n", p=P)
                    sp.dma_start(chunk(s).rearrange("p (b n) -> p b n", b=2), src).then_inc(slot_full[s], 16)

            def expert(e, k, turn):
                for i in range(CHUNKS):
                    need = CHUNKS * k + i - SLOTS + 1
                    if need > 0:
                        sp.wait_ge(slots_used, turn * (UNROLL * CHUNKS) + need)
                    elif need + FIRST_CHUNK > 0:
                        held_by = PIECES[(need + FIRST_CHUNK - 1) // 2]
                        sp.wait_ge(*released[held_by])
                    elif slot_of(k, i) in last_use:
                        for used in last_use[slot_of(k, i)]:
                            sp.wait_ge(*used)
                    load_chunk(e, i, slot_of(k, i))

            experts(sp, expert, peel=UNROLL)

            def extra(e, r, o):
                sp.wait_ge(slots_used, o * CHUNKS + CHUNKS * E)
                for i in range(CHUNKS):
                    load_chunk(e, i, slot_of(E, i))

            extras(sp, extra)
            for t in range(TB):
                sp.wait_ge(result_ready, t + 1)
                sp.dma_start(out[0, t * P:(t + 1) * P, :], result[:, t, :]).then_inc(result_out, 16)
            sp.wait_ge(result_out, 16 * TB)

        @block.gpsimd
        def _(pool):
            nc.gpsimd.memset(ident[:, :], 0.0).then_inc(ident_step, 1)
            pool.wait_ge(ident_step, 1)
            nc.gpsimd.affine_select(out=ident[:, :], in_=ident[:, :], compare_op=ALU.not_equal, fill=1.0,
                                    base=0, pattern=[[-1, P]], channel_multiplier=1).then_inc(ident_ready, 1)
            nc.gpsimd.memset(u_pad[:, :, 0:PAD], 0.0).then_inc(pads_ready, 1)
            nc.gpsimd.memset(mean_w[:, :], 1.0 / D_CONV).then_inc(consts_ready, 1)
            nc.gpsimd.memset(ones_b[:, :], 1.0).then_inc(consts_ready, 1)
            nc.gpsimd.memset(ident_b[:, :], 0.0).then_inc(consts_step, 1)
            nc.gpsimd.memset(causal[:, :], 0.0).then_inc(consts_step, 1)
            nc.gpsimd.memset(upto[:, :], 1.0).then_inc(consts_step, 1)
            nc.gpsimd.memset(bias_sel[:, :, :], 0.0).then_inc(consts_step, 1)
            pool.wait_ge(consts_step, 4)
            nc.gpsimd.affine_select(out=ident_b[:, :], in_=ident_b[:, :], compare_op=ALU.not_equal, fill=1.0,
                                    base=0, pattern=[[-1, P]], channel_multiplier=1).then_inc(consts_ready, 1)
            nc.gpsimd.affine_select(out=causal[:, :], in_=causal[:, :], compare_op=ALU.is_ge, fill=MASK_VALUE,
                                    base=0, pattern=[[-1, P]], channel_multiplier=1).then_inc(consts_ready, 1)
            nc.gpsimd.affine_select(out=upto[:, :], in_=upto[:, :], compare_op=ALU.is_ge, fill=0.0,
                                    base=0, pattern=[[1, P]], channel_multiplier=-1).then_inc(consts_ready, 1)
            pool.wait_ge(consts_ready, 5)
            nc.gpsimd.iota(count_i, pattern=[[1, SEQ]], base=1, channel_multiplier=0).then_inc(count_step, 1)
            pool.wait_ge(count_step, 1)
            nc.gpsimd.tensor_copy(count[:, :], count_i).then_inc(count_ready, 1)
            nc.gpsimd.memset(place[:, :, E:E + 1], 0.0).then_inc(count_ready, 1)
            nc.gpsimd.memset(weighted[:, :, :], 0.0).then_inc(count_ready, 1)
            pool.wait_ge(count_ready, 3)
            pool.wait_ge(xn_turned, 4)
            nc.gpsimd.memset(k_aug[DH:P, :, :], 0.0).then_inc(aug_zeroed, 1)
            pool.wait_ge(aug_zeroed, 1)
            nc.gpsimd.memset(k_aug[DH:DH + 1, :, :], 1.0).then_inc(aug_zeroed, 1)
            pool.wait_ge(aug_zeroed, 2)
            pool.wait_ge(x_added, 1)
            nc.gpsimd.memset(q_aug[DH:96, :, :], 1.0).then_inc(aug_zeroed, 1)
            pool.wait_ge(aug_zeroed, 3)
            nc.gpsimd.memset(q_aug[96:P, :, :], 0.0).then_inc(aug_zeroed, 1)
            pool.wait_ge(aug_zeroed, 4)
            flat = bgu_parts[:, :, :].rearrange("p g n -> p (g n)")
            for n, (rows, casts) in enumerate(((slice(32, 64), 1), (slice(64, 96), 1), (slice(64, 96), 3))):
                pool.wait_ge(bgu_cast, casts)
                nc.gpsimd.tensor_tensor(bgu_raw[rows, :], bgu_raw[rows, :], flat[rows, :], ALU.subtract).then_inc(bgu_rest, 1)
                pool.wait_ge(bgu_rest, n + 1)
            for part in range(3):
                view = bias_sel[:, :, :].rearrange("p e (h c) -> p e h c", h=2)
                nc.gpsimd.affine_select(out=view, in_=view, compare_op=ALU.not_equal, fill=1.0, base=-32 * part,
                                        pattern=[[-2, E // 2], [-1, 2], [0, CAP]], channel_multiplier=1)\
                    .then_inc(bias_sel_ready, 1)
                pool.wait_ge(bias_sel_ready, part + 1)
            pool.wait_ge(att_done, len(GROUPS))
            nc.gpsimd.memset(bdown_sb, 0.0).then_inc(moe_zeroed, 1)
            pool.wait_ge(h_done, TB)
            nc.gpsimd.memset(gates_t, 0.0).then_inc(moe_zeroed, 1)

        @block.scalar
        def _(act):
            act.dma_start(wf_sb[:, :, :], w_in[:, F_COL:F_COL + HEADS].rearrange("(k p) n -> p k n", p=P)).then_inc(wf_in, 16)
            act.dma_start(bf_col[:, :], b_f.rearrange("(a b) -> a b", b=1)).then_inc(bf_in, 16)

            def mean_square(src, junk, into, done):
                nc.scalar.activation(junk, src, ACT.Square, accum_out=into).then_inc(done, 1)

            for t in range(TB):
                act.wait_ge(x_in[t], 16)
                mean_square(x_sb[:, t, :], xn[:, t, :], stat[:, t:t + 1], x_squared)
            for t in range(TB):
                act.wait_ge(x_mean, t + 1)
                nc.scalar.activation(stat[:, 4 + t:5 + t], stat[:, 2 + t:3 + t], ACT.Sqrt).then_inc(x_root, 1)
            act.dma_start(wr_sb[:, :, :], w_router.rearrange("(k p) n -> p k n", p=P)).then_inc(router_in, 16)
            act.dma_start(br_row[:, :], b_router.partition_broadcast(P)).then_inc(router_in, 16)

            act.wait_ge(proj_done, 1)
            act.wait_ge(bf_in, 16)
            nc.scalar.activation(fg[:, 0, :], work[0:HEADS, 0, 0:SEQ], ACT.Identity, bias=bf_col[:, :]).then_inc(proj_copied, 1)
            act.wait_ge(fg_step, 1)
            nc.scalar.activation(fg[:, 2, :], fg[:, 1, :], ACT.Exp).then_inc(decay_exp, 1)
            act.wait_ge(fg_step, 2)
            nc.scalar.activation(fg[:, 4, :], fg[:, 3, :], ACT.Ln).then_inc(decay_exp, 1)
            act.wait_ge(cols_ready, 2)
            act.wait_ge(pads_ready, 1)
            flat = bgu_parts[:, :, :].rearrange("p g n -> p (g n)")
            for c in range(CB):
                act.wait_ge(proj_done, 2 + c)
                nc.scalar.activation(conv_y[:, c, :], work[:, (1 + c) % 4, SEQ:2 * SEQ], ACT.Sigmoid,
                                     bias=cols[:, B_G + c:B_G + c + 1])
                nc.scalar.activation(u_pad[:, c, PAD:PAD + SEQ], work[:, (1 + c) % 4, 0:SEQ], ACT.Identity,
                                     bias=cols[:, B_A + c:B_A + c + 1]).then_inc(proj_copied, 1)
                if c == 1:
                    act.wait_ge(bgu_in, 16 * 12)
                    nc.scalar.activation(flat[0:96, :], bgu_raw[0:96, :], ACT.Copy).then_inc(bgu_cast, 1)
            act.wait_ge(decay_ready, 2)
            act.wait_ge(aug_zeroed, 4)
            act.dma_start(q_aug[DH:DH + 1, :, :], fg[:, 2, :]).then_inc(decay_in, 16)
            act.dma_start(k_aug[DH + 1:DH + 2, :, :], fg[:, 3, :]).then_inc(decay_in, 16)
            for rows, rests in ((slice(32, 64), 1), (slice(64, 96), 2)):
                act.wait_ge(bgu_rest, rests)
                nc.scalar.activation(flat[rows, :], bgu_raw[rows, :], ACT.Copy).then_inc(bgu_cast, 1)

            def split_heads(n):
                dst, first = (q_aug if n < 8 else k_aug), 4 * (n % 2)
                act.wait_ge(proj_done, n)
                for odd in range(2):
                    h = first + odd
                    done = nc.scalar.activation(
                        dst[0:DH, h:h + 3:2, :],
                        work[DH * odd:DH * odd + DH, BANK_OF[n], :].rearrange("p (c t) -> p c t", c=2), ACT.Copy)
                done.then_inc(proj_copied, 1)

            split_heads(6)
            act.wait_ge(bgu_rest, 3)
            nc.scalar.activation(flat[64:96, :], bgu_raw[64:96, :], ACT.Copy).then_inc(bgu_cast, 1)
            for n in range(7, 10):
                split_heads(n)

            def copy_values(n):
                act.wait_ge(proj_done, n)
                nc.scalar.activation(v_sb[:, n - 10, :], work[:, BANK_OF[n], :], ACT.Copy).then_inc(proj_copied, 1)

            copy_values(10)
            act.wait_ge(centred, 1)
            nc.scalar.activation(ln_tmp, conv_y, ACT.Square).then_inc(squared, 1)
            copy_values(11)
            act.wait_ge(var_ready, 1)
            nc.scalar.activation(ln_s[:, 1, :], ln_s[:, 0, :], ACT.Sqrt).then_inc(root_ready, 1)

            def exps(g):
                heads = GROUPS[g][1]
                act.wait_ge(max_ready, g + 1)
                if g >= 2:
                    act.wait_ge(probs_turned, g - 1)
                w = 512 // len(heads)
                for n in range(len(heads)):
                    done = nc.scalar.activation(probs[:, g % 2, n * w:(n + 1) * w], work[:, S_BANKS[g % 2], n * w:(n + 1) * w],
                                                ACT.Exp, scale=SCALE, bias=amax[:, g, n:n + 1], accum_out=asum[:, g, n:n + 1])
                done.then_inc(exp_done, 1)

            def copy_output(qb):
                act.wait_ge(att_done, 2 if qb == 0 else len(GROUPS))
                nc.scalar.activation(att_y[:, :, qb * P:(qb + 1) * P], work[:, O_BANK, :].rearrange("p (k t) -> p k t", k=4),
                                     ACT.Copy).then_inc(att_copied, 1)

            exps(0)
            exps(1)
            act.wait_ge(normed, 1)
            for c in range(CB):
                done = nc.scalar.activation(ln_tmp[:, c, :], conv_y[:, c, :], ACT.Sigmoid,
                                            scale=cols[:, LN_G + c:LN_G + c + 1], bias=cols[:, LN_B + c:LN_B + c + 1])
            done.then_inc(swish_sig, 1)
            exps(2)
            exps(3)
            copy_output(0)
            for g in range(4, len(GROUPS)):
                exps(g)
            copy_output(1)

            act.wait_ge(moe_zeroed, 1)
            act.dma_start(bdown_sb[0:E, :], b_down).then_inc(bdown_in, 16)

            def block_stats(t):
                act.wait_ge(h_copied, t + 1)
                mean_square(hn[:, t, :], part_junk(t), stat[:, 8 + t:9 + t], h_squared)
                act.wait_ge(h_mean, t + 1)
                nc.scalar.activation(stat[:, 12 + t:13 + t], stat[:, 10 + t:11 + t], ACT.Sqrt).then_inc(h_root, 1)

            def part_junk(t):
                return region_m[:, 0 if t == 0 else T1_PARTS:][:, 0:1024]

            def cast_part(t, n):
                act.wait_ge(hn_ready if n == 0 else part_dve, t + 1 if n == 0 else 2 * t + 1)
                nc.scalar.activation(hn_parts[t][:, n, :], hn[:, t, :], ACT.Copy).then_inc(part_act, 1)

            def copy_logits(t):
                act.wait_ge(logits_done, t + 1)
                nc.scalar.activation(logits_t[:, t * P:(t + 1) * P], work[0:E, 3, t * P:(t + 1) * P], ACT.Copy)\
                    .then_inc(logits_t_ready, 1)

            block_stats(0)
            cast_part(0, 0)
            cast_part(0, 1)
            copy_logits(0)
            block_stats(1)
            copy_logits(1)
            cast_part(1, 0)
            cast_part(1, 1)
            act.wait_ge(logits_done, TB)
            act.dma_start(final_gain, norm_final_g.partition_broadcast(P)).then_inc(final_gain_in, 16)
            act.wait_ge(top_diff, 1)
            nc.scalar.activation(top_w[:, 1, :, :], top_w[:, 0, :, :], ACT.Exp).then_inc(top_exp, 1)
            act.wait_ge(gates_turned, 1)
            act.wait_ge(moe_zeroed, 2)
            nc.scalar.activation(gates_t[0:E, :], work[0:E, GATE_BANK, 0:SEQ], ACT.Copy).then_inc(gates_t_ready, 1)

            def expert_pass(n):
                act.wait_ge(gate_clamped, n + 1)
                nc.scalar.activation(sig_h, gate_h, ACT.Sigmoid, scale=SWIGLU_ALPHA).then_inc(sig_ready, 1)
                act.wait_ge(weighted_turned, n + 1)
                nc.scalar.activation(scatter_flat, work[:, TURN_BANK, :], ACT.Copy).then_inc(scatter_ready, 1)
                act.wait_ge(act_turned, n + 1)
                nc.scalar.activation(act_t_flat, work[:, TURN_BANK, :], ACT.Copy).then_inc(act_t_ready, 1)
                act.wait_ge(slots_used, n * CHUNKS + CHUNKS)
                nc.scalar.activation(y_sb, work[:, OUT_BANK, :], ACT.Copy).then_inc(y_ready, 1)

            experts(act, lambda e, k, turn: expert_pass(e))
            total = extras(act, lambda e, r, o: expert_pass(o + E))
            nc.scalar.activation(stat[:, 15:16], stat[:, 14:15], ACT.Sqrt).then_inc(o_root, 1)
            for t in range(TB):
                act.wait_ge(scattered, total * (TB * (SEQ // CAP - 1)) + (TB * (E - 1) + t + 1))
                mean_square(resid[:, t, :], squares, stat[:, t:t + 1], o_squared)
                act.wait_ge(o_mean, t + 1)
                nc.scalar.activation(stat[:, 4 + t:5 + t], stat[:, 2 + t:3 + t], ACT.Sqrt).then_inc(o_root, 1)

        @block.vector
        def _(dve):
            V = nc.vector

            def inv_rms(n, src, mid, into, squared_sem, mean_sem, root_sem, scale_sem, roots_before=0):
                dve.wait_ge(squared_sem, n + 1)
                V.tensor_scalar(mid[0], src, 1.0 / D, RMS_EPS, ALU.mult, ALU.add).then_inc(mean_sem, 1)
                dve.wait_ge(root_sem, n + 1 + roots_before)
                V.reciprocal(into, mid[1]).then_inc(scale_sem, 1)
                dve.wait_ge(scale_sem, n + 1)

            for t in range(TB):
                inv_rms(t, stat[:, t:t + 1], (stat[:, 2 + t:3 + t], stat[:, 4 + t:5 + t]), stat[:, 6 + t:7 + t],
                        x_squared, x_mean, x_root, x_scale)
                V.tensor_scalar(xn[:, t, :], x_sb[:, t, :], stat[:, 6 + t:7 + t], None, ALU.mult).then_inc(xn_ready, 1)
            dve.wait_ge(vecs_turned, 1)
            V.tensor_copy(cols[:, :], work[:, 3, 0:36]).then_inc(cols_ready, 1)
            V.tensor_copy(dw_cols[:, :, :], work[:, 3, 64:64 + 32 * CB].rearrange("p (c j) -> p c j", c=CB)[:, :, 0:TAPS])\
                .then_inc(cols_ready, 1)
            dve.wait_ge(cols_ready, 2)
            for n in range(4):
                t, g = n // 2, n % 2
                dve.wait_ge(xn_turned, n + 1)
                V.tensor_tensor(xn_t[:, 4 * g:4 * g + 4, t * P:(t + 1) * P], work[:, n, :].rearrange("p (k t) -> p k t", k=4),
                                cols[:, G_MIX + 4 * g:G_MIX + 4 * g + 4].unsqueeze(2).to_broadcast([P, 4, P]),
                                ALU.mult).then_inc(xnt_ready, 1)

            dve.wait_ge(proj_copied, 1)
            V.scalar_tensor_tensor(fg[:, 1, :], fg[:, 0, :], -1.0, fg[:, 0, :], ALU.mult, ALU.min).then_inc(fg_step, 1)
            dve.wait_ge(decay_exp, 1)
            V.tensor_scalar(fg[:, 3, :], fg[:, 2, :], 1.0, None, ALU.add).then_inc(fg_step, 1)
            dve.wait_ge(decay_exp, 2)
            V.scalar_tensor_tensor(fg[:, 5, :], fg[:, 0, :], 0.0, fg[:, 4, :], ALU.min, ALU.subtract).then_inc(fg_step, 1)
            V.memset(fg[:, 1, :], 1.0).then_inc(fg_step, 1)
            dve.wait_ge(fg_step, 4)
            V.tensor_tensor_scan(fg[:, 4, :], fg[:, 1, :], fg[:, 5, :], 0.0, ALU.mult, ALU.add).then_inc(fg_step, 1)
            dve.wait_ge(fg_step, 5)
            V.tensor_scalar(fg[:, 2, :], fg[:, 4, :], 1.0 / SCALE, None, ALU.mult).then_inc(decay_ready, 1)
            V.tensor_scalar(fg[:, 3, :], fg[:, 4, :], -1.0 / SCALE, None, ALU.mult).then_inc(decay_ready, 1)

            OPS = TAPS + 1
            with dve.Fori(0, CB) as c:
                dve.wait_ge(proj_copied, c + 2)
                V.tensor_tensor(u_pad[:, c, PAD:PAD + SEQ], u_pad[:, c, PAD:PAD + SEQ], conv_y[:, c, :], ALU.mult).then_inc(u_ready, 1)
                dve.wait_ge(u_ready, c + 1)
                for j in range(TAPS):
                    acc = conv_y[:, c, :] if j % 2 == 0 else conv_b
                    src, w = u_pad[:, c, j:j + SEQ], dw_cols[:, c, j:j + 1]
                    if j == 0:
                        done = V.tensor_scalar(acc, src, w, cols[:, bass.ds(c + B_DW, 1)], ALU.mult, ALU.add)
                    elif j == 1:
                        done = V.tensor_scalar(acc, src, w, None, ALU.mult)
                    else:
                        dve.wait_ge(tap_done, c * OPS + (j - 1))
                        done = V.scalar_tensor_tensor(acc, src, w, acc, ALU.mult, ALU.add)
                    done.then_inc(tap_done, 1)
                dve.wait_ge(tap_done, c * OPS + TAPS)
                V.tensor_tensor(conv_y[:, c, :], conv_y[:, c, :], conv_b, ALU.add).then_inc(tap_done, 1)

            dve.wait_ge(mean_done, 1)
            V.tensor_tensor(conv_y, conv_y, work[:, MEAN_BANK, 0:SEQ].unsqueeze(1).to_broadcast([P, CB, SEQ]), ALU.subtract)\
                .then_inc(centred, 1)
            dve.wait_ge(var_done, 1)
            V.tensor_scalar(ln_s[:, 0, :], work[:, VAR_BANK, 0:SEQ], LN_EPS, None, ALU.add).then_inc(var_ready, 1)

            def row_max(g):
                heads = GROUPS[g][1]
                w = 512 // len(heads)
                dve.wait_ge(scores_done, g + 1)
                V.reduce_max(amax[:, g, 0:len(heads)], work[:, S_BANKS[g % 2], :].rearrange("p (n w) -> p n w", w=w),
                             AX.X).then_inc(max_step, 1)
                dve.wait_ge(max_step, g + 1)
                V.tensor_scalar(amax[:, g, 0:len(heads)], amax[:, g, 0:len(heads)], -SCALE, None, ALU.mult)\
                    .then_inc(max_ready, 1)

            def normalise(g):
                heads = GROUPS[g][1]
                w = 512 // len(heads)
                n = len(heads)
                dve.wait_ge(exp_done, g + 1)
                V.reciprocal(asum[:, g, 0:n], asum[:, g, 0:n]).then_inc(sum_step, 1)
                dve.wait_ge(sum_step, g + 1)
                view = probs[:, g % 2, :].rearrange("p (n w) -> p n w", w=w)
                V.tensor_tensor(view, view, asum[:, g, 0:n].unsqueeze(2).to_broadcast([P, n, w]), ALU.mult)\
                    .then_inc(probs_ready, 1)

            def copy_turned(g):
                dve.wait_ge(probs_turned, g + 1)
                if g >= 2:
                    dve.wait_ge(att_done, g - 1)
                V.tensor_copy(probs_t[:, g % 2, :], work[:, T_BANK, :]).then_inc(probs_t_ready, 1)

            row_max(0)
            dve.wait_ge(root_ready, 1)
            V.reciprocal(ln_s[:, 0, :], ln_s[:, 1, :]).then_inc(ln_step, 1)
            row_max(1)
            normalise(0)
            dve.wait_ge(ln_step, 1)
            V.tensor_tensor(conv_y, conv_y, ln_s[:, 0, :].unsqueeze(1).to_broadcast([P, CB, SEQ]), ALU.mult)\
                .then_inc(normed, 1)
            row_max(2)
            normalise(1)
            copy_turned(0)
            dve.wait_ge(swish_sig, 1)
            for c in range(CB):
                V.tensor_scalar(conv_y[:, c, :], conv_y[:, c, :], cols[:, LN_G + c:LN_G + c + 1],
                                cols[:, LN_B + c:LN_B + c + 1], ALU.mult, ALU.add).then_inc(ln_step, 1)
            dve.wait_ge(ln_step, 1 + CB)
            V.tensor_tensor(conv_y, conv_y, ln_tmp, ALU.mult).then_inc(conv_ready, 1)
            for g in range(3, len(GROUPS) + 2):
                if g < len(GROUPS):
                    row_max(g)
                if g <= len(GROUPS):
                    normalise(g - 1)
                copy_turned(g - 2)

            steps = [0]

            def then(ins):
                steps[0] += 1
                ins.then_inc(top_step, 1)
                dve.wait_ge(top_step, steps[0])

            dve.wait_ge(count_ready, 3)
            then(V.tensor_scalar(expert_no[:, :], count[:, 0:E], -1.0, None, ALU.add))
            dve.wait_ge(router_in, 32)

            def copy_h(t):
                dve.wait_ge(h_done, t + 1)
                V.tensor_copy(hn[:, t, :], resid[:, t, :]).then_inc(h_copied, 1)

            def copy_h_turned(t):
                for g in range(2):
                    dve.wait_ge(h_turned, 2 * t + g + 1)
                    V.tensor_tensor(h_t[:, 4 * g:4 * g + 4, t * P:(t + 1) * P], work[:, 1 + g, :].rearrange("p (k t) -> p k t", k=4),
                                    cols[:, G_FFN + 4 * g:G_FFN + 4 * g + 4].unsqueeze(2).to_broadcast([P, 4, P]),
                                    ALU.mult).then_inc(ht_ready, 1)

            def scale_h(t):
                inv_rms(t, stat[:, 8 + t:9 + t], (stat[:, 10 + t:11 + t], stat[:, 12 + t:13 + t]), stat[:, 14 + t:15 + t],
                        h_squared, h_mean, h_root, h_scale)
                V.tensor_scalar(hn[:, t, :], hn[:, t, :], stat[:, 14 + t:15 + t], None, ALU.mult).then_inc(hn_ready, 1)

            def less_part(t, n):
                dve.wait_ge(part_act, 2 * t + n + 1)
                V.tensor_tensor(hn[:, t, :] if n == 0 else hn_parts[t][:, 2, :], hn[:, t, :], hn_parts[t][:, n, :],
                                ALU.subtract).then_inc(part_dve, 1)

            def choose(t):
                dve.wait_ge(logits_turned, t + 1)
                then(V.scalar_tensor_tensor(logits[:, t, :], work[:, 0, t * E:(t + 1) * E], stat[:, 14 + t:15 + t], br_row[:, :],
                                            ALU.mult, ALU.add))
                then(V.max(out=top8[:, t, :], in_=logits[:, t, :]))
                then(V.max_index(out=top8_i[:, t, :], in_max=top8[:, t, :], in_values=logits[:, t, :]))
                then(V.tensor_copy(top_i[:, t, :], top8_i[:, t, 0:TOP_K]))
                then(V.tensor_tensor(onehot[:, 0, t, :, :], expert_no[:, :].unsqueeze(1).to_broadcast([P, TOP_K, E]),
                                     top_i[:, t, :].unsqueeze(2).to_broadcast([P, TOP_K, E]), ALU.is_equal))
                then(V.tensor_reduce(chosen[:, t, :], onehot[:, 0, t, :, :].rearrange("p k e -> p e k"), AX.X, ALU.add))
                V.tensor_copy(chosen_b[:, t, :], chosen[:, t, :]).then_inc(chosen_ready, 1)

            copy_h(0)
            copy_h_turned(0)
            scale_h(0)
            less_part(0, 0)
            less_part(0, 1)
            choose(0)
            copy_h(1)
            copy_h_turned(1)
            scale_h(1)
            choose(1)
            less_part(1, 0)
            less_part(1, 1)
            dve.wait_ge(places_done, 1)
            V.tensor_tensor(place[:, :, 0:E], work[:, TURN_BANK, 0:TB * E].rearrange("p (t e) -> p t e", t=TB), chosen[:, :, :],
                            ALU.mult).then_inc(place_ready, 1)
            dve.wait_ge(place_ready, 1)

            def select_tokens(e, r, g):
                dve.wait_ge(gathered, g)
                for t in range(TB):
                    done = V.tensor_scalar(select[:, t, :], count[:, bass.ds(r * CAP, CAP)], place[:, t, bass.ds(e, 1)], None,
                                           ALU.is_equal)
                done.then_inc(select_ready, 1)

            def weigh_tokens(e, r, g):
                dve.wait_ge(gathered, g + 1)
                for t in range(TB):
                    done = V.tensor_scalar(weighted[:, t, CAP:2 * CAP], count[:, bass.ds(r * CAP, CAP)],
                                           place[:, t, bass.ds(e, 1)], gates[:, t, bass.ds(e, 1)], ALU.is_equal, ALU.mult)
                done.then_inc(weighted_ready, 1)

            def expert_pass(n):
                dve.wait_ge(slots_used, n * CHUNKS + UP_CHUNKS)
                V.tensor_scalar(gate_h, work[:, GATE_BANK, :], SWIGLU_LIMIT, None, ALU.min).then_inc(gate_clamped, 1)
                V.tensor_scalar(up_h, work[:, UP_BANK, :], SWIGLU_LIMIT, -SWIGLU_LIMIT, ALU.min, ALU.max).then_inc(up_clamped, 1)
                dve.wait_ge(gate_clamped, n + 1)
                dve.wait_ge(sig_ready, n + 1)
                V.tensor_tensor(sig_h, sig_h, gate_h, ALU.mult).then_inc(glu_ready, 1)
                dve.wait_ge(glu_ready, n + 1)
                dve.wait_ge(up_clamped, n + 1)
                V.scalar_tensor_tensor(up_h, up_h, 1.0, sig_h, ALU.add, ALU.mult).then_inc(act_ready, 1)

            def copy_tokens(g):
                dve.wait_ge(gathered, g + 1)
                V.tensor_tensor(tok_t, work[:, OUT_BANK, :].rearrange("p (k c) -> p k c", k=KB),
                                cols[:, G_FFN:G_FFN + KB].unsqueeze(2).to_broadcast([P, KB, CAP]), ALU.mult).then_inc(tok_t_ready, 1)

            select_tokens(0, 0, 0)
            V.tensor_tensor(top_w[:, 0, :, :], top8[:, :, 0:TOP_K], top8[:, :, 0:1].to_broadcast([P, TB, TOP_K]),
                            ALU.subtract).then_inc(top_diff, 1)
            dve.wait_ge(top_exp, 1)
            then(V.reduce_sum(top_s[:, 0, :], top_w[:, 1, :, :], AX.X))
            then(V.reciprocal(top_s[:, 1, :], top_s[:, 0, :]))
            then(V.tensor_tensor(top_w[:, 2, :, :], top_w[:, 1, :, :], top_s[:, 1, :].unsqueeze(2).to_broadcast([P, TB, TOP_K]),
                                 ALU.mult))
            for t in range(TB):
                then(V.tensor_tensor(onehot[:, 1, t, :, :], onehot[:, 0, t, :, :],
                                     top_w[:, 2, t, :].unsqueeze(2).to_broadcast([P, TOP_K, E]), ALU.mult))
            V.tensor_reduce(gates[:, :, :], onehot[:, 1, :, :, :].rearrange("p t k e -> p t e k"), AX.X, ALU.add)\
                .then_inc(gates_ready, 1)
            dve.wait_ge(gates_ready, 1)
            copy_tokens(0)
            then(V.tensor_scalar(over_f[:, 0, :], work[0:1, TURN_BANK, TB * E:TB * E + E], float(CAP), None, ALU.is_gt))
            then(V.memset(over_f[:, 3, :], 1.0))
            then(V.tensor_tensor_scan(over_f[:, 1, :], over_f[:, 3, :], over_f[:, 0, :], 0.0, ALU.mult, ALU.add))
            then(V.tensor_tensor(over_f[:, 2, :], over_f[:, 1, :], over_f[:, 0, :], ALU.subtract))
            then(V.tensor_copy(over[:, 0, :], over_f[:, 0, :]))
            then(V.tensor_copy(over[:, 1, :], over_f[:, 2, :]))
            V.tensor_copy(over_all[:, :], over_f[:, 1, E - 1:E]).then_inc(over_ready, 1)

            def expert(e, k, turn):
                weigh_tokens(e, 0, e)
                select_tokens(e + 1, 0, e + 1)
                expert_pass(e)
                copy_tokens(e + 1)

            experts(dve, expert)

            def extra(e, r, o):
                select_tokens(e, r, o + (E + 1))
                copy_tokens(o + (E + 1))
                weigh_tokens(e, r, o + (E + 1))
                expert_pass(o + E)

            extras(dve, extra)
            dve.wait_ge(final_gain_in, 16)
            for t in range(TB):
                inv_rms(t, stat[:, t:t + 1], (stat[:, 2 + t:3 + t], stat[:, 4 + t:5 + t]), stat[:, 6 + t:7 + t],
                        o_squared, o_mean, o_root, o_scale, roots_before=1)
                V.scalar_tensor_tensor(result[:, t, :], resid[:, t, :], stat[:, 6 + t:7 + t], final_gain,
                                       ALU.mult, ALU.mult).then_inc(result_ready, 1)

        @block.tensor
        def _(pe):
            def mm(out_, lhsT, rhs, start, stop):
                return nc.tensor.matmul(out_, lhsT, rhs, start=start, stop=stop, skip_group_check=True)

            pe.wait_ge(ident_ready, 1)
            pe.wait_ge(vecs_in, 16 * 6)
            nc.tensor.transpose(work[:, 3, 0:36], vec_rows, ident[0:36, 0:36])
            pe.wait_ge(dw_in, 16)
            for c in range(CB):
                last = nc.tensor.transpose(work[:, 3, 64 + 32 * c:64 + 32 * c + TAPS], dw_rows[:, c * P:(c + 1) * P],
                                           ident[0:TAPS, 0:TAPS])
            last.then_inc(vecs_turned, 1)
            for n in range(4):
                t, g = n // 2, n % 2
                pe.wait_ge(xn_ready, t + 1)
                if n == 3:
                    pe.wait_ge(cols_ready, 2)
                for j in range(4):
                    last = nc.tensor.transpose(work[:, n, j * P:(j + 1) * P], xn[:, t, (4 * g + j) * P:(4 * g + j + 1) * P], ident[:, :])
                last.then_inc(xn_turned, 1)
            for t in range(TB):
                for h in range(2):
                    last = mm(resid[:, t, h * HALF:(h + 1) * HALF], ident[:, :], x_sb[:, t, h * HALF:(h + 1) * HALF], True, False)
            last.then_inc(x_added, 1)

            def arrived(name):
                pe.wait_ge(slot_full[2 * PIECES.index(name)], 16)

            def columns(bank, at, name, c):
                for kb in range(KB):
                    last = mm(work[:, bank, at:at + SEQ], piece(name)[:, kb, c * P:(c + 1) * P], xn_t[:, kb, :], kb == 0, kb == KB - 1)
                return last

            pe.wait_ge(xnt_ready, 4)
            pe.wait_ge(wf_in, 16)
            for kb in range(KB):
                last = mm(work[0:HEADS, 0, 0:SEQ], wf_sb[:, kb, :], xn_t[:, kb, :], kb == 0, kb == KB - 1)
            last.then_inc(proj_done, 1)
            arrived("glu_a")
            arrived("glu_g")
            for c in range(CB):
                if c == 3:
                    pe.wait_ge(proj_copied, 1)
                columns(BANK_OF[2 + c], 0, "glu_a", c)
                last = columns(BANK_OF[2 + c], SEQ, "glu_g", c)
                last.then_inc(proj_done, 1)
            for n in range(6, 10):
                name = "q" if n < 8 else "k"
                if n % 2 == 0:
                    arrived(name)
                pe.wait_ge(proj_copied, n - 4)
                columns(BANK_OF[n], 0, name, 2 * (n % 2))
                last = columns(BANK_OF[n], SEQ, name, 2 * (n % 2) + 1)
                last.then_inc(proj_done, 1)

            def values(n):
                for kb in range(KB):
                    last = mm(work[:, BANK_OF[n], :], xn_t[:, kb, (n - 10) * P:(n - 9) * P], piece("v")[:, kb, :], kb == 0, kb == KB - 1)
                last.then_inc(proj_done, 1)

            arrived("v")
            pe.wait_ge(proj_copied, 6)
            values(10)
            pe.wait_ge(consts_ready, 5)
            pe.wait_ge(tap_done, CB * (TAPS + 1))
            pe.wait_ge(proj_copied, 7)
            for c in range(CB):
                last = mm(work[:, MEAN_BANK, 0:SEQ], mean_w[:, :], conv_y[:, c, :], c == 0, c == CB - 1)
            last.then_inc(mean_done, 1)
            pe.wait_ge(proj_copied, 8)
            values(11)
            pe.wait_ge(proj_copied, 9)
            pe.wait_ge(squared, 1)
            for c in range(CB):
                last = mm(work[:, VAR_BANK, 0:SEQ], mean_w[:, :], ln_tmp[:, c, :], c == 0, c == CB - 1)
            last.then_inc(var_done, 1)

            def scores(g):
                qb, heads = GROUPS[g]
                bank, w = S_BANKS[g % 2], 512 // len(heads)
                if g >= 2:
                    pe.wait_ge(exp_done, g - 1)
                keys = (qb + 1) * P
                for n, h in enumerate(heads):
                    mm(work[:, bank, n * w:n * w + keys], q_aug[:, h, qb * P:(qb + 1) * P], k_aug[:, h, 0:keys], True, False)
                    last = mm(work[:, bank, n * w + qb * P:n * w + keys], ident_b[:, :], causal[:, :], False, True)
                last.then_inc(scores_done, 1)

            def turn(g):
                pe.wait_ge(probs_ready, g + 1)
                if g >= 1:
                    pe.wait_ge(probs_t_ready, g)
                else:
                    pe.wait_ge(proj_copied, 11)
                for b in range(4):
                    last = nc.tensor.transpose(work[:, T_BANK, b * P:(b + 1) * P], probs[:, g % 2, b * P:(b + 1) * P], ident[:, :])
                last.then_inc(probs_turned, 1)

            def weigh_values(g):
                qb, heads = GROUPS[g]
                pe.wait_ge(probs_t_ready, g + 1)
                if g == 2:
                    pe.wait_ge(att_copied, 1)
                b = 0
                for h in heads:
                    to = work[DH * (h % 2):DH * (h % 2) + DH, O_BANK, (h // 2) * P:(h // 2 + 1) * P]
                    for s in range(qb + 1):
                        last = mm(to, v_sb[:, s, h * DH:(h + 1) * DH], probs_t[:, g % 2, b * P:(b + 1) * P], s == 0, s == qb)
                        b += 1
                last.then_inc(att_done, 1)

            def project(name, t, h):
                for kb in range(4):
                    last = mm(resid[:, t, h * HALF:(h + 1) * HALF],
                              (conv_y if name == "out_conv" else att_y)[:, kb, t * P:(t + 1) * P],
                              piece(name)[:, kb, h * HALF:(h + 1) * HALF], False, False)
                return last

            pe.wait_ge(decay_in, 32)
            pe.wait_ge(proj_copied, 10)
            scores(0)
            scores(1)
            turn(0)
            scores(2)
            pe.wait_ge(var_ready, 1)
            weigh_values(0)
            turn(1)
            scores(3)
            weigh_values(1)
            fill = [("out_conv", 0, 0), ("out_conv", 0, 1), ("out_att", 0, 0), ("out_att", 0, 1),
                    ("out_conv", 1, 0), ("out_conv", 1, 1)]
            pe.wait_ge(conv_ready, 1)
            arrived("out_conv")
            arrived("out_att")

            def fill_in(count_):
                for _ in range(count_):
                    name, t, h = fill.pop(0)
                    if (name, t, h) == ("out_att", 0, 0):
                        pe.wait_ge(att_copied, 1)
                    last = project(name, t, h)
                    if (name, t, h) == ("out_att", 0, 1):
                        last.then_inc(h_done, 1)
                    if (name, t, h) == ("out_conv", 1, 1):
                        last.then_inc(conv_added, 1)

            fill_in(1)
            turn(2)
            scores(4)
            fill_in(1)
            weigh_values(2)
            turn(3)
            scores(5)
            fill_in(1)
            weigh_values(3)
            turn(4)
            fill_in(1)
            weigh_values(4)
            turn(5)
            fill_in(1)
            weigh_values(5)
            fill_in(1)

            def turn_h(t):
                pe.wait_ge(h_copied, t + 1)
                if t == 0:
                    pe.wait_ge(exp_done, len(GROUPS))
                for g in range(2):
                    if t > 0:
                        pe.wait_ge(ht_ready, g + 1)
                    for j in range(4):
                        last = nc.tensor.transpose(work[:, 1 + g, j * P:(j + 1) * P], hn[:, t, (4 * g + j) * P:(4 * g + j + 1) * P], ident[:, :])
                    last.then_inc(h_turned, 1)

            def route(t):
                pe.wait_ge(ht_ready, 2 * t + 2)
                if t == 0:
                    pe.wait_ge(probs_t_ready, len(GROUPS))
                else:
                    pe.wait_ge(logits_t_ready, t)
                for kb in range(KB):
                    last = mm(work[0:E, 3, t * P:(t + 1) * P], wr_sb[:, kb, :], h_t[:, kb, t * P:(t + 1) * P], kb == 0, kb == KB - 1)
                last.then_inc(logits_done, 1)

            def turn_logits(t):
                pe.wait_ge(logits_t_ready, t + 1)
                if t > 0:
                    pe.wait_ge(chosen_ready, t)
                nc.tensor.transpose(work[:, 0, t * E:(t + 1) * E], logits_t[:, t * P:(t + 1) * P], ident[0:E, 0:E])\
                    .then_inc(logits_turned, 1)

            pe.wait_ge(router_in, 32)
            turn_h(0)
            pe.wait_ge(att_copied, 2)
            project("out_att", 1, 0)
            route(0)
            last = project("out_att", 1, 1)
            last.then_inc(h_done, 1)
            turn_logits(0)
            turn_h(1)
            route(1)
            turn_logits(1)
            pe.wait_ge(chosen_ready, TB)
            for t in range(TB):
                for s in range(t + 1):
                    mm(work[:, TURN_BANK, t * E:(t + 1) * E], (upto if s == t else ones_b)[:, :], chosen_b[:, s, :], s == 0, s == t)
            for s in range(TB):
                last = mm(work[0:1, TURN_BANK, TB * E:TB * E + E], ones_b[:, 0:1], chosen_b[:, s, :], s == 0, s == TB - 1)
            last.then_inc(places_done, 1)

            def gather(g):
                pe.wait_ge(select_ready, g + 1)
                for kb in range(KB):
                    for n in range(3 * TB):
                        last = mm(work[:, OUT_BANK, kb * CAP:(kb + 1) * CAP], hn_parts[n // 3][:, n % 3, kb * P:(kb + 1) * P],
                                  select[:, n // 3, :], n == 0, n == 3 * TB - 1)
                last.then_inc(gathered, 1)

            def add_bdown():
                pe.wait_ge(bdown_in, 16)
                for t in range(TB):
                    for h in range(2):
                        mm(resid[:, t, h * HALF:(h + 1) * HALF], gates_t[:, t * P:(t + 1) * P], bdown_sb[:, h * HALF:(h + 1) * HALF], False, False)

            def slot_arrived(k, i, turn):
                pe.wait_ge(slot_full[slot_of(k, i)], turn * (16 * ROUNDS) + 16 * uses_of(k, i))

            def expert_pass(e, n, g, next_g, arrived_chunk, slot, is_first=False):
                pe.wait_ge(tok_t_ready, g + 1)
                for bank in (GATE_BANK, UP_BANK):
                    mm(work[:, bank, :], bias_sel[:, e // 2, :], bgu_parts[:, e % 2, bank * 512:(bank + 1) * 512], True, False)
                for kb in range(KB):
                    arrived_chunk(kb)
                    w = chunk(slot(kb))
                    for bank in (GATE_BANK, UP_BANK):
                        for h in range(2):
                            c = bank * D_FF + h * HALF
                            last = mm(work[CAP * h:CAP * (h + 1), bank, :], tok_t[:, kb, :], w[:, c:c + HALF], False, kb == KB - 1)
                    last.then_inc(slots_used, 1)
                pe.wait_ge(weighted_ready, n + 1)
                for h in range(2):
                    for t in range(TB):
                        last = nc.tensor.transpose(work[:, TURN_BANK, (h * TB + t) * P:(h * TB + t + 1) * P],
                                                   weighted[:, t, (1 - h) * CAP:(1 - h) * CAP + P], ident[:, :])
                last.then_inc(weighted_turned, 1)
                if next_g is not None:
                    gather(next_g)
                if is_first:
                    add_bdown()
                pe.wait_ge(act_ready, n + 1)
                pe.wait_ge(scatter_ready, n + 1)
                for j in range(4):
                    last = nc.tensor.transpose(work[:, TURN_BANK, j * P:(j + 1) * P], up_h[:, j * P:(j + 1) * P], ident[:, :])
                last.then_inc(act_turned, 1)
                pe.wait_ge(act_t_ready, n + 1)
                if next_g is not None:
                    pe.wait_ge(tok_t_ready, next_g + 1)
                for m in range(DOWN_CHUNKS):
                    arrived_chunk(UP_CHUNKS + m)
                    w = chunk(slot(UP_CHUNKS + m))
                    for b in range(2):
                        f = 2 * m + b
                        lhsT = act_t[:, f % 4, (f // 4) * CAP:(f // 4 + 1) * CAP]
                        for h in range(2):
                            last = mm(work[CAP * h:CAP * (h + 1), OUT_BANK, :], lhsT, w[:, b * D + h * HALF:b * D + (h + 1) * HALF],
                                      f == 0, f == FB - 1)
                    last.then_inc(slots_used, 1)
                pe.wait_ge(y_ready, n + 1)
                for t in range(TB):
                    for h in range(2):
                        last = mm(resid[:, t, h * HALF:(h + 1) * HALF], scatter_sb[:, h * TB + t, :], y_sb, False, False)
                    last.then_inc(scattered, 1)

            pe.wait_ge(part_dve, 2 * TB)
            pe.wait_ge(count_ready, 3)
            gather(0)
            pe.wait_ge(gates_ready, 1)
            for t in range(TB):
                last = nc.tensor.transpose(work[0:E, GATE_BANK, t * P:(t + 1) * P], gates[:, t, :], ident[:, :])
            last.then_inc(gates_turned, 1)
            pe.wait_ge(gates_t_ready, 1)
            pe.wait_ge(bias_sel_ready, 3)
            pe.wait_ge(bgu_cast, 4)
            experts(pe, lambda e, k, turn: expert_pass(e, e, e, e + 1, lambda i: slot_arrived(k, i, turn), lambda i: slot_of(k, i),
                                                       is_first=(k == 0 and LOOP_FROM > 0)))

            def extra(e, r, o):
                gather(o + (E + 1))
                expert_pass(e, o + E, o + (E + 1), None,
                            lambda i: pe.wait_ge(slot_full[slot_of(E, i)], o * 16 + 16 * uses_of(E, i)), lambda i: slot_of(E, i))

            extras(pe, extra)


_INS = ["x", "norm_mix_g", "w_in", "b_f", "b_glu", "w_dw", "b_dw", "ln_g", "ln_b", "w_out", "norm_ffn_g",
        "w_router", "b_router", "w_gu", "b_gu", "w_down", "b_down", "norm_final_g"]


def kernel(**inputs):
    import concourse.bacc as bacc
    from concourse.bass_utils import run_bass_kernel_spmd

    nc = bacc.Bacc("TRN2", target_bir_lowering=False, num_devices=1, dynamic_dma_scratch_size=1024)
    arrays, args = {}, []
    for name in _INS:
        a = np.ascontiguousarray(inputs[name])
        arrays[f"in_{name}"] = a
        args.append(nc.dram_tensor(f"in_{name}", a.shape, mybir.dt.from_np(a.dtype), kind="ExternalInput").ap())
    result = nc.dram_tensor("result", inputs["x"].shape, F32, kind="ExternalOutput").ap()
    hybrid_layer(nc, *args, result)
    return run_bass_kernel_spmd(nc, [arrays], core_ids=[0]).results[0]["result"]
```

```python
from contextlib import ExitStack

import concourse.bass as bass
import numpy as np
from concourse import mybir

F32 = mybir.dt.float32
BF16 = mybir.dt.bfloat16
I32 = mybir.dt.int32
U32 = mybir.dt.uint32
ALU = mybir.AluOpType
ACT = mybir.ActivationFunctionType
AX = mybir.AxisListType

P = 128
TOP_K = 4
Q_BLOCK = 128
SWIGLU_LIMIT = 7.0
SWIGLU_ALPHA = 1.702
RMS_EPS = 1e-6
LN_EPS = 1e-5
MASK_VALUE = -1e30

SLOTS = 21
SLOT = 2048
CAP = 64


def hybrid_layer(nc, x, norm_mix_g, w_in, b_f, b_glu, w_dw, b_dw, ln_g, ln_b, w_out, norm_ffn_g,
                 w_router, b_router, w_gu, b_gu, w_down, b_down, norm_final_g, out):
    _, SEQ, D = x.shape
    HEADS = b_f.shape[0]
    D_CONV = b_dw.shape[0]
    D_ATT = D - D_CONV
    DH = D_ATT // HEADS
    TAPS = w_dw.shape[0]
    E = w_router.shape[1]
    D_FF = w_down.shape[1]
    TB = SEQ // P
    KB = D // P
    CB = D_CONV // P
    FB = D_FF // P
    HALF = D // 2
    PAD = TAPS - 1
    SCALE = float(DH) ** -0.5
    assert SEQ == 2 * P == 2 * Q_BLOCK and D == D_FF == 1024 and D_ATT == D_CONV == HALF == 512
    assert DH == 64 and SEQ % CAP == 0 and E <= P

    PIECES = ["glu_a", "glu_g", "q", "k", "v", "out_conv", "out_att"]
    PIECE_COLS = {"q": 0, "k": D_ATT, "v": 2 * D_ATT,
                  "glu_a": 3 * D_ATT + HEADS, "glu_g": 3 * D_ATT + HEADS + D_CONV}
    F_COL = 3 * D_ATT
    FIRST_PIECE = SLOTS - 2 - 2 * len(PIECES)
    UP_CHUNKS, DOWN_CHUNKS = KB, FB // 2
    CHUNKS = UP_CHUNKS + DOWN_CHUNKS
    assert FIRST_PIECE == 5

    UNROLL = next(u for u in range(1, E + 1) if u * CHUNKS % SLOTS == 0)
    LOOP_FROM = E % UNROLL
    LOOPS = E // UNROLL
    assert LOOP_FROM > 0
    ROUNDS = UNROLL * CHUNKS // SLOTS

    def slot_of(e, i):
        return (CHUNKS * e + i) % SLOTS

    def uses_of(e, i):
        s = slot_of(e, i)
        piece_before = FIRST_PIECE <= s < SLOTS - 2 and ((s - FIRST_PIECE) % 2 == 0 or s < FIRST_PIECE + 4)
        return int(piece_before) + (CHUNKS * e + i) // SLOTS + 1

    GROUPS = [(0, [0, 1, 2, 3]), (0, [4, 5, 6, 7])] + [(1, [h, h + 1]) for h in range(0, HEADS, 2)]

    with ExitStack() as ctx:
        def sb(name, shape, dt):
            return ctx.enter_context(nc.sbuf_tensor(name, shape, dt))

        def sem(name):
            return ctx.enter_context(nc.semaphore(name))

        ring = sb("ring", [P, (SLOTS - 1) * SLOT], F32)

        region_q = sb("region_q", [P, 2048], F32)
        region_k = sb("region_k", [P, 2048], F32)
        region_x = sb("region_x", [P, 2048], F32)
        region_m = sb("region_m", [P, 4224], F32)
        CONV_Y, T1_PARTS = 2176, 1536

        x_sb = region_q[:, :].rearrange("p (t d) -> p t d", t=TB)
        q_aug = region_q[:, :].rearrange("p (h t) -> p h t", h=HEADS)
        hn = region_q[:, :].rearrange("p (t d) -> p t d", t=TB)
        gate_h, sig_h, up_h = (region_q[:, 512 * n:512 * (n + 1)] for n in range(3))
        result = hn

        xn = region_k[:, :].rearrange("p (t d) -> p t d", t=TB)
        k_aug = region_k[:, :].rearrange("p (h t) -> p h t", h=HEADS)
        h_t = region_k[:, :].rearrange("p (k t) -> p k t", k=KB)

        xn_t = region_x[:, :].rearrange("p (k t) -> p k t", k=KB)
        late_probs = region_x[:, 0:1024].rearrange("p (b n) -> p b n", b=2)
        probs_t = region_x[:, 1024:2048].rearrange("p (b n) -> p b n", b=2)
        tok_t = region_x[:, 0:512].rearrange("p (k c) -> p k c", k=KB)
        act_t_flat, y_sb, scatter_flat = (region_x[:, 512 * n:512 * (n + 1)] for n in (1, 2, 3))
        act_t = act_t_flat.rearrange("p (j n) -> p j n", j=4)
        scatter_sb = scatter_flat.rearrange("p (j n) -> p j n", j=4)
        bdown_sb = region_x[:, 512:1536]

        DECAY_SLOT, BGU_SLOT, ROWS_SLOT, X_SLOT = 2, 3, 4, SLOTS - 1
        vec_rows = ring[0:36, ROWS_SLOT * SLOT:ROWS_SLOT * SLOT + P]
        dw_rows = ring[0:TAPS, ROWS_SLOT * SLOT + P:ROWS_SLOT * SLOT + P + D_CONV]
        fg = ring[0:HEADS, DECAY_SLOT * SLOT:DECAY_SLOT * SLOT + 6 * SEQ].rearrange("p (n t) -> p n t", n=6)
        count_i = ring[:, DECAY_SLOT * SLOT + 6 * SEQ:DECAY_SLOT * SLOT + 7 * SEQ].bitcast(I32)
        bgu_raw = ring[:, BGU_SLOT * SLOT:(BGU_SLOT + 1) * SLOT]
        x_again = ring[:, (X_SLOT - 1) * SLOT:X_SLOT * SLOT].rearrange("p (t d) -> p t d", t=TB)

        v_sb = region_m[:, 0:1024].rearrange("p (s n) -> p s n", s=TB)
        u_pad = region_m[:, 1024:1024 + CB * (SEQ + PAD)].rearrange("p (c t) -> p c t", c=CB)
        ln_tmp = region_m[:, 1024:2048].rearrange("p (c t) -> p c t", c=CB)
        conv_y = region_m[:, CONV_Y:CONV_Y + 1024].rearrange("p (c t) -> p c t", c=CB)
        att_y = region_m[:, CONV_Y + 1024:CONV_Y + 2048].rearrange("p (c t) -> p c t", c=CB)
        conv_pool = ring[:, ROWS_SLOT * SLOT + 1024:(ROWS_SLOT + 1) * SLOT].rearrange("p (c t) -> p c t", c=CB)
        conv_odd = region_m[:, CONV_Y + 1024:CONV_Y + 2048].rearrange("p (c t) -> p c t", c=CB)
        early_probs = region_m[:, CONV_Y + 1024:CONV_Y + 2048].rearrange("p (b n) -> p b n", b=2)
        hn_parts = [region_m[:, at:at + 1536].bitcast(BF16).rearrange("p (s d) -> p s d", s=3) for at in (0, T1_PARTS)]
        final_gain = region_m[:, CONV_Y + 1024:CONV_Y + 2048]

        bgu_parts = sb("bgu_parts", [96, 2, 1024], BF16)
        bias_sel = sb("bias_sel", [96, E // 2, P], BF16)
        ident = sb("ident", [P, P], F32)
        ident_b = sb("ident_b", [P, P], BF16)
        causal = sb("causal", [P, P], BF16)
        upto = sb("upto", [P, P], BF16)
        ones_b = sb("ones_b", [P, P], BF16)
        mean_w = sb("mean_w", [P, P], F32)
        count = sb("count", [P, SEQ], F32)
        expert_no = sb("expert_no", [P, E], F32)
        cols = sb("cols", [P, 36], F32)
        dw_cols = sb("dw_cols", [P, CB, TAPS], F32)
        G_MIX, B_A, B_G, B_DW, LN_G, LN_B, G_FFN = 0, 8, 12, 16, 20, 24, 28
        wf_sb = sb("wf_sb", [P, KB, HEADS], F32)
        bf_col = sb("bf_col", [HEADS, 1], F32)
        wr_sb = sb("wr_sb", [P, KB, E], F32)
        br_row = sb("br_row", [P, E], F32)
        stat = sb("stat", [P, 16], F32)
        spare = sb("spare", [P, 3 * SEQ], F32)
        ln_s = spare[:, SEQ:3 * SEQ].rearrange("p (n t) -> p n t", n=2)
        product = spare[:, 0:SEQ]
        channel_sum = ln_s[:, 1, :]
        logits_t = spare[0:E, 0:SEQ]
        gates_t = spare[:, 0:SEQ]
        onehot = spare[:, SEQ:SEQ + 2 * TB * TOP_K * E].rearrange("p (n t k e) -> p n t k e", n=2, t=TB, k=TOP_K)
        amax = sb("amax", [P, len(GROUPS), 4], F32)
        asum = sb("asum", [P, len(GROUPS), 4], F32)
        logits = sb("logits", [P, TB, E], F32)
        top8 = sb("top8", [P, TB, 8], F32)
        top8_i = sb("top8_i", [P, TB, 8], U32)
        top_i = sb("top_i", [P, TB, TOP_K], F32)
        top_w = sb("top_w", [P, 3, TB, TOP_K], F32)
        top_s = sb("top_s", [P, 2, TB], F32)
        chosen = sb("chosen", [P, TB, E], F32)
        chosen_b = sb("chosen_b", [P, TB, E], BF16)
        gates = sb("gates", [P, TB, E], F32)
        place = sb("place", [P, TB, E + 1], F32)
        over_f = sb("over_f", [1, 4, E], F32)
        over = sb("over", [1, 2, E], I32)
        over_all = sb("over_all", [1, 1], I32)
        select = sb("select", [P, TB, CAP], BF16)
        weighted = sb("weighted", [P, TB, 3 * CAP], F32)

        resid = ctx.enter_context(nc.psum_tensor("resid", [P, TB, D], F32))
        work = ctx.enter_context(nc.psum_tensor("work", [P, 4, 512], F32))
        GATE_BANK, UP_BANK, TURN_BANK, OUT_BANK = range(4)
        S_BANKS, T_BANK, O_BANK = (2, 1), 3, 0

        x_in = [sem(f"x_in{t}") for t in range(TB)]
        vecs_in, dw_in, wf_in, bf_in = sem("vecs_in"), sem("dw_in"), sem("wf_in"), sem("bf_in")
        bgu_in, router_in, final_gain_in = sem("bgu_in"), sem("router_in"), sem("final_gain_in")
        x_again_in, bdown_in, decay_in, result_out = sem("x_again_in"), sem("bdown_in"), sem("decay_in"), sem("result_out")
        slot_full = [sem(f"slot_full{s}") for s in range(SLOTS)]
        slots_used = sem("slots_used")
        ident_step, ident_ready, consts_step, consts_ready = sem("ident_step"), sem("ident_ready"), sem("consts_step"), sem("consts_ready")
        count_step, count_ready, aug_zeroed = sem("count_step"), sem("count_ready"), sem("aug_zeroed")
        bias_sel_ready, bgu_cast, bgu_rest, pads_ready, moe_zeroed = sem("bias_sel_ready"), sem("bgu_cast"), sem("bgu_rest"), sem("pads_ready"), sem("moe_zeroed")
        x_squared, x_mean, x_root, x_scale, xn_ready = sem("x_squared"), sem("x_mean"), sem("x_root"), sem("x_scale"), sem("xn_ready")
        vecs_turned, cols_ready, xn_turned, xnt_ready, x_added = sem("vecs_turned"), sem("cols_ready"), sem("xn_turned"), sem("xnt_ready"), sem("x_added")
        proj_done, proj_copied, u_ready = sem("proj_done"), sem("proj_copied"), sem("u_ready")
        taps_started, pool_taps, sum_cleared, tap_done, fg_step, decay_exp, decay_ready = sem("taps_started"), sem("pool_taps"), sem("sum_cleared"), sem("tap_done"), sem("fg_step"), sem("decay_exp"), sem("decay_ready")
        mean_done, centred, squared, squares_summed, var_done, var_ready, root_ready = sem("mean_done"), sem("centred"), sem("squared"), sem("squares_summed"), sem("var_done"), sem("var_ready"), sem("root_ready")
        ln_step, normed, swish_sig, conv_ready = sem("ln_step"), sem("normed"), sem("swish_sig"), sem("conv_ready")
        scores_done, max_step, max_ready, exp_done, sum_step, probs_ready = sem("scores_done"), sem("max_step"), sem("max_ready"), sem("exp_done"), sem("sum_step"), sem("probs_ready")
        probs_turned, probs_t_ready, att_done, att_copied = sem("probs_turned"), sem("probs_t_ready"), sem("att_done"), sem("att_copied")
        conv_added, h_done, h_copied, h_squared, h_mean, h_root, h_scale = sem("conv_added"), sem("h_done"), sem("h_copied"), sem("h_squared"), sem("h_mean"), sem("h_root"), sem("h_scale")
        h1_copied, h_turned, ht_ready = sem("h1_copied"), sem("h_turned"), sem("ht_ready")
        part_act, part_dve, part_pool = sem("part_act"), sem("part_dve"), sem("part_pool")
        logits_done, logits_t_ready, logits_turned = sem("logits_done"), sem("logits_t_ready"), sem("logits_turned")
        top_step, top_diff, top_exp, gates_ready = sem("top_step"), sem("top_diff"), sem("top_exp"), sem("gates_ready")
        logits_scaled, largest_ready, onehot_ready = sem("logits_scaled"), sem("largest_ready"), sem("onehot_ready")
        choice_ready, chosen_ready = sem("choice_ready"), sem("chosen_ready")
        places_done, gates_turned, gates_t_ready, place_ready, over_ready = sem("places_done"), sem("gates_turned"), sem("gates_t_ready"), sem("place_ready"), sem("over_ready")
        select_ready, gathered, tok_t_ready = sem("select_ready"), sem("gathered"), sem("tok_t_ready")
        weighted_ready, weighted_turned, scatter_ready = sem("weighted_ready"), sem("weighted_turned"), sem("scatter_ready")
        gate_clamped, up_clamped, sig_ready, glu_ready, act_ready = sem("gate_clamped"), sem("up_clamped"), sem("sig_ready"), sem("glu_ready"), sem("act_ready")
        act_turned, act_t_ready, y_ready, scattered = sem("act_turned"), sem("act_t_ready"), sem("y_ready"), sem("scattered")
        o_squared, o_mean, o_root, o_scale, result_ready = sem("o_squared"), sem("o_mean"), sem("o_root"), sem("o_scale"), sem("result_ready")

        FIRST = 7
        OPS = TAPS - FIRST + 3
        POOL_STEPS = 2 * (FIRST - 2) - 1

        BANK_OF = {n: (n - 1) % 4 for n in range(1, 10)} | {10: 1, 11: 3}
        MEAN_BANK, VAR_BANK = 2, 0
        HALVES = 2 * TB
        HT_BANKS = ((1, 2), (0, 1))
        LOGITS_BANKS, CHOICE_BANKS = (3, 2), (0, 1)

        def first_slot(name):
            return FIRST_PIECE + 2 * PIECES.index(name)

        def piece(name):
            s = first_slot(name)
            view = ring[:, s * SLOT:(s + 2) * SLOT]
            return view.rearrange("p (k n) -> p k n", k=4 if name.startswith("out") else KB)

        def chunk(s):
            if s == SLOTS - 2:
                return region_k[:, :]
            at = min(s, SLOTS - 2) * SLOT
            return ring[:, at:at + SLOT]

        def probs(g):
            return (early_probs if g < 2 else late_probs)[:, g % 2, :]

        def experts(eng, one, peel=0):
            first = LOOP_FROM + peel
            for e in range(first):
                one(e, e, 0)
            with eng.Fori(0, LOOPS - peel // UNROLL) as turn:
                for u in range(UNROLL):
                    one(turn * UNROLL + (first + u), first + u, turn)

        def experts_over(eng):
            eng.wait_ge(over_ready, 1)
            return eng.value_load(over_all[0:1, 0:1], min_val=0, max_val=E)

        def extras(eng, one, total):
            with eng.If(total > 0):
                with eng.Fori(0, E) as e:
                    more = eng.value_load(over[0:1, 0, bass.ds(e, 1)], min_val=0, max_val=1)
                    before = eng.value_load(over[0:1, 1, bass.ds(e, 1)], min_val=0, max_val=E)
                    with eng.If(more > 0):
                        with eng.Fori(0, SEQ // CAP - 1) as r:
                            one(e, r + 1, before * (SEQ // CAP - 1) + r)

        block = ctx.enter_context(nc.Block())

        @block.sync
        def _(sp):
            for t in range(TB):
                sp.dma_start(x_sb[:, t, :], x[0, t * P:(t + 1) * P, :]).then_inc(x_in[t], 16)
            at = 0
            for vec, n in ((norm_mix_g, KB), (b_glu, 2 * CB), (b_dw, CB), (ln_g, CB), (ln_b, CB), (norm_ffn_g, KB)):
                sp.dma_start(vec_rows[at:at + n, :], vec.rearrange("(a p) -> a p", p=P)).then_inc(vecs_in, 16)
                at += n
            sp.dma_start(dw_rows, w_dw).then_inc(dw_in, 16)
            for half in range(2):
                for name in PIECES[:2]:
                    c = PIECE_COLS[name] + 256 * half
                    src = w_in[:, c:c + 256].rearrange("(k p) n -> p k n", p=P)
                    sp.dma_start(piece(name)[:, :, 256 * half:256 * half + 256], src).then_inc(slot_full[first_slot(name) + half], 16)
            for name in PIECES[2:]:
                s = first_slot(name)
                if name.startswith("out"):
                    first = D_ATT if name == "out_conv" else 0
                    src = w_out[first:first + HALF, :].rearrange("(k p) n -> p k n", p=P)
                else:
                    c = PIECE_COLS[name]
                    src = w_in[:, c:c + 512].rearrange("(k p) n -> p k n", p=P)
                sp.dma_start(piece(name), src).then_inc(slot_full[s], 16)
                if name == "q":
                    src = b_gu.rearrange("(e g) (u h n) -> g u e h n", g=2, u=2, h=2)
                    for part in range(3):
                        for g in range(2):
                            for u in range(2):
                                c = (2 * g + u) * HALF
                                sp.dma_start(bgu_raw[32 * part:32 * part + 32, c:c + HALF], src[g, u]).then_inc(bgu_in, 16)

            sp.dma_start(x_again, x[0, :, :].rearrange("(t p) d -> p t d", p=P)).then_inc(x_again_in, 16)

            released = {"glu_a": (proj_done, 5), "glu_g": (proj_done, 5), "q": (proj_done, 7), "k": (proj_done, 9),
                        "v": (proj_done, 11), "out_conv": (conv_added, 1), "out_att": (h_done, 3)}

            last_use = {ROWS_SLOT: ((vecs_turned, 1), (tap_done, CB * OPS)), DECAY_SLOT: ((decay_in, 32), (count_ready, 1)),
                        BGU_SLOT: ((bgu_cast, 4),), X_SLOT: ((x_added, 1),), SLOTS - 2: ((logits_done, TB),)}

            def load_chunk(e, i, s):
                if i < UP_CHUNKS:
                    sp.dma_start(chunk(s), w_gu[e, i * P:(i + 1) * P, :]).then_inc(slot_full[s], 16)
                else:
                    j = 2 * (i - UP_CHUNKS)
                    src = w_down[e, j * P:(j + 2) * P, :].rearrange("(b p) n -> p b n", p=P)
                    sp.dma_start(chunk(s).rearrange("p (b n) -> p b n", b=2), src).then_inc(slot_full[s], 16)

            def expert(e, k, turn):
                for i in range(CHUNKS):
                    number = CHUNKS * k + i
                    if number >= SLOTS:
                        sp.wait_ge(slots_used, turn * (UNROLL * CHUNKS) + number - SLOTS + 1)
                    elif number in last_use:
                        for used in last_use[number]:
                            sp.wait_ge(*used)
                    elif number >= FIRST_PIECE:
                        sp.wait_ge(*released[PIECES[(number - FIRST_PIECE) // 2]])
                    load_chunk(e, i, slot_of(k, i))

            experts(sp, expert, peel=UNROLL)

            def extra(e, r, o):
                sp.wait_ge(slots_used, o * CHUNKS + CHUNKS * E)
                for i in range(CHUNKS):
                    load_chunk(e, i, slot_of(E, i))

            extras(sp, extra, experts_over(sp))
            for n in range(HALVES):
                t, half = n // 2, slice(n % 2 * HALF, (n % 2 + 1) * HALF)
                sp.wait_ge(result_ready, n + 1)
                sp.dma_start(out[0, t * P:(t + 1) * P, half], result[:, t, half]).then_inc(result_out, 16)
            sp.wait_ge(result_out, 16 * HALVES)

        @block.gpsimd
        def _(pool):
            nc.gpsimd.memset(ident[:, :], 0.0).then_inc(ident_step, 1)
            pool.wait_ge(ident_step, 1)
            nc.gpsimd.affine_select(out=ident[:, :], in_=ident[:, :], compare_op=ALU.not_equal, fill=1.0,
                                    base=0, pattern=[[-1, P]], channel_multiplier=1).then_inc(ident_ready, 1)
            nc.gpsimd.memset(u_pad[:, :, 0:PAD], 0.0).then_inc(pads_ready, 1)
            nc.gpsimd.memset(mean_w[:, :], 1.0 / D_CONV).then_inc(consts_ready, 1)
            nc.gpsimd.memset(ones_b[:, :], 1.0).then_inc(consts_ready, 1)
            nc.gpsimd.memset(ident_b[:, :], 0.0).then_inc(consts_step, 1)
            nc.gpsimd.memset(causal[:, :], 0.0).then_inc(consts_step, 1)
            nc.gpsimd.memset(upto[:, :], 1.0).then_inc(consts_step, 1)
            nc.gpsimd.memset(bias_sel[:, :, :], 0.0).then_inc(consts_step, 1)
            pool.wait_ge(consts_step, 4)
            nc.gpsimd.affine_select(out=ident_b[:, :], in_=ident_b[:, :], compare_op=ALU.not_equal, fill=1.0,
                                    base=0, pattern=[[-1, P]], channel_multiplier=1).then_inc(consts_ready, 1)
            nc.gpsimd.affine_select(out=causal[:, :], in_=causal[:, :], compare_op=ALU.is_ge, fill=MASK_VALUE,
                                    base=0, pattern=[[-1, P]], channel_multiplier=1).then_inc(consts_ready, 1)
            nc.gpsimd.affine_select(out=upto[:, :], in_=upto[:, :], compare_op=ALU.is_ge, fill=0.0,
                                    base=0, pattern=[[1, P]], channel_multiplier=-1).then_inc(consts_ready, 1)
            pool.wait_ge(consts_ready, 5)
            nc.gpsimd.iota(count_i, pattern=[[1, SEQ]], base=1, channel_multiplier=0).then_inc(count_step, 1)
            pool.wait_ge(count_step, 1)
            nc.gpsimd.tensor_copy(count[:, :], count_i).then_inc(count_ready, 1)
            nc.gpsimd.memset(place[:, :, E:E + 1], 0.0).then_inc(count_ready, 1)
            nc.gpsimd.memset(weighted[:, :, :], 0.0).then_inc(count_ready, 1)
            pool.wait_ge(count_ready, 3)
            pool.wait_ge(xn_turned, 4)
            nc.gpsimd.memset(k_aug[DH:P, :, :], 0.0).then_inc(aug_zeroed, 1)
            pool.wait_ge(aug_zeroed, 1)
            nc.gpsimd.memset(k_aug[DH:DH + 1, :, :], 1.0).then_inc(aug_zeroed, 1)
            pool.wait_ge(aug_zeroed, 2)
            pool.wait_ge(xn_ready, TB)
            nc.gpsimd.memset(q_aug[DH:96, :, :], 1.0).then_inc(aug_zeroed, 1)
            pool.wait_ge(aug_zeroed, 3)
            nc.gpsimd.memset(q_aug[96:P, :, :], 0.0).then_inc(aug_zeroed, 1)
            pool.wait_ge(aug_zeroed, 4)
            flat = bgu_parts[:, :, :].rearrange("p g n -> p (g n)")

            def glu(c):
                pool.wait_ge(proj_copied, c + 2)
                nc.gpsimd.tensor_tensor(u_pad[:, c, PAD:PAD + SEQ], u_pad[:, c, PAD:PAD + SEQ], conv_y[:, c, :], ALU.mult)\
                    .then_inc(u_ready, 1)
                pool.wait_ge(u_ready, c + 1)

            def less_bgu_part(n, rows, casts):
                pool.wait_ge(bgu_cast, casts)
                nc.gpsimd.tensor_tensor(bgu_raw[rows, :], bgu_raw[rows, :], flat[rows, :], ALU.subtract).then_inc(bgu_rest, 1)
                pool.wait_ge(bgu_rest, n + 1)

            def convolve(c):
                for j in range(2, FIRST):
                    to = conv_pool[:, c, :] if j == 2 else product
                    nc.gpsimd.tensor_tensor(to, u_pad[:, c, j:j + SEQ], dw_cols[:, c, j:j + 1].to_broadcast([P, SEQ]), ALU.mult)\
                        .then_inc(pool_taps, 1)
                    if j > 2:
                        pool.wait_ge(pool_taps, c * POOL_STEPS + 2 * (j - 2))
                        nc.gpsimd.tensor_tensor(conv_pool[:, c, :], conv_pool[:, c, :], product, ALU.add).then_inc(pool_taps, 1)
                        pool.wait_ge(pool_taps, c * POOL_STEPS + 2 * (j - 2) + 1)

            glu(0)
            convolve(0)
            glu(1)
            convolve(1)
            less_bgu_part(0, slice(32, 64), 1)
            glu(2)
            convolve(2)
            less_bgu_part(1, slice(64, 96), 1)
            glu(3)
            convolve(3)
            less_bgu_part(2, slice(64, 96), 3)
            for part in range(3):
                view = bias_sel[:, :, :].rearrange("p e (h c) -> p e h c", h=2)
                nc.gpsimd.affine_select(out=view, in_=view, compare_op=ALU.not_equal, fill=1.0, base=-32 * part,
                                        pattern=[[-2, E // 2], [-1, 2], [0, CAP]], channel_multiplier=1)\
                    .then_inc(bias_sel_ready, 1)
                pool.wait_ge(bias_sel_ready, part + 1)
            pool.wait_ge(att_done, len(GROUPS))
            nc.gpsimd.memset(bdown_sb, 0.0).then_inc(moe_zeroed, 1)

            def third_part(t):
                pool.wait_ge(part_act, 2 * t + 2)
                nc.gpsimd.tensor_tensor(hn_parts[t][:, 2, :], hn[:, t, :], hn_parts[t][:, 1, :], ALU.subtract).then_inc(part_pool, 1)

            third_part(0)
            pool.wait_ge(logits_turned, TB)
            nc.gpsimd.memset(gates_t, 0.0).then_inc(moe_zeroed, 1)
            third_part(1)

        @block.scalar
        def _(act):
            act.dma_start(wf_sb[:, :, :], w_in[:, F_COL:F_COL + HEADS].rearrange("(k p) n -> p k n", p=P)).then_inc(wf_in, 16)
            act.dma_start(bf_col[:, :], b_f.rearrange("(a b) -> a b", b=1)).then_inc(bf_in, 16)

            def mean_square(src, junk, into, done):
                nc.scalar.activation(junk, src, ACT.Square, accum_out=into).then_inc(done, 1)

            act.wait_ge(ident_ready, 1)
            nc.scalar.activation(stat[:, 15:16], ident[:, 0:1], ACT.Sqrt)
            for t in range(TB):
                act.wait_ge(x_in[t], 16)
                mean_square(x_sb[:, t, :], xn[:, t, :], stat[:, t:t + 1], x_squared)
                act.wait_ge(x_mean, t + 1)
                nc.scalar.activation(stat[:, 4 + t:5 + t], stat[:, 2 + t:3 + t], ACT.Sqrt).then_inc(x_root, 1)
            act.wait_ge(vecs_turned, 1)
            nc.scalar.activation(cols[:, :], work[:, 3, 0:36], ACT.Copy).then_inc(cols_ready, 1)
            nc.scalar.activation(dw_cols[:, :, :], work[:, 3, 64:64 + 32 * CB].rearrange("p (c j) -> p c j", c=CB)[:, :, 0:TAPS],
                                 ACT.Copy).then_inc(cols_ready, 1)
            act.dma_start(wr_sb[:, :, :], w_router.rearrange("(k p) n -> p k n", p=P)).then_inc(router_in, 16)
            act.dma_start(br_row[:, :], b_router.partition_broadcast(P)).then_inc(router_in, 16)

            act.wait_ge(proj_done, 1)
            act.wait_ge(bf_in, 16)
            nc.scalar.activation(fg[:, 0, :], work[0:HEADS, 0, 0:SEQ], ACT.Identity, bias=bf_col[:, :]).then_inc(proj_copied, 1)
            act.wait_ge(fg_step, 1)
            nc.scalar.activation(fg[:, 2, :], fg[:, 1, :], ACT.Exp).then_inc(decay_exp, 1)
            act.wait_ge(fg_step, 2)
            nc.scalar.activation(fg[:, 4, :], fg[:, 3, :], ACT.Ln).then_inc(decay_exp, 1)
            act.wait_ge(cols_ready, 2)
            act.wait_ge(pads_ready, 1)
            flat = bgu_parts[:, :, :].rearrange("p g n -> p (g n)")
            for c in range(CB):
                act.wait_ge(proj_done, 2 + c)
                nc.scalar.activation(conv_y[:, c, :], work[:, (1 + c) % 4, SEQ:2 * SEQ], ACT.Sigmoid,
                                     bias=cols[:, B_G + c:B_G + c + 1])
                nc.scalar.activation(u_pad[:, c, PAD:PAD + SEQ], work[:, (1 + c) % 4, 0:SEQ], ACT.Identity,
                                     bias=cols[:, B_A + c:B_A + c + 1]).then_inc(proj_copied, 1)
                act.wait_ge(u_ready, c + 1)
                nc.scalar.activation(conv_y[:, c, :], u_pad[:, c, 0:SEQ], ACT.Identity, scale=dw_cols[:, c, 0:1],
                                     bias=cols[:, B_DW + c:B_DW + c + 1]).then_inc(taps_started, 1)
                nc.scalar.activation(conv_odd[:, c, :], u_pad[:, c, 1:1 + SEQ], ACT.Copy, scale=dw_cols[:, c, 1:2]).then_inc(taps_started, 1)
                if c == 1:
                    act.wait_ge(bgu_in, 16 * 12)
                    nc.scalar.activation(flat[0:96, :], bgu_raw[0:96, :], ACT.Copy).then_inc(bgu_cast, 1)
            act.wait_ge(decay_ready, 2)
            act.wait_ge(aug_zeroed, 4)
            act.dma_start(q_aug[DH:DH + 1, :, :], fg[:, 2, :]).then_inc(decay_in, 16)
            act.dma_start(k_aug[DH + 1:DH + 2, :, :], fg[:, 3, :]).then_inc(decay_in, 16)
            for rows, rests in ((slice(32, 64), 1), (slice(64, 96), 2)):
                act.wait_ge(bgu_rest, rests)
                nc.scalar.activation(flat[rows, :], bgu_raw[rows, :], ACT.Copy).then_inc(bgu_cast, 1)

            def split_heads(n):
                dst, first = (q_aug if n < 8 else k_aug), 4 * (n % 2)
                act.wait_ge(proj_done, n)
                for odd in range(2):
                    h = first + odd
                    done = nc.scalar.activation(
                        dst[0:DH, h:h + 3:2, :],
                        work[DH * odd:DH * odd + DH, BANK_OF[n], :].rearrange("p (c t) -> p c t", c=2), ACT.Copy)
                done.then_inc(proj_copied, 1)

            split_heads(6)
            act.wait_ge(bgu_rest, 3)
            nc.scalar.activation(flat[64:96, :], bgu_raw[64:96, :], ACT.Copy).then_inc(bgu_cast, 1)
            split_heads(7)
            split_heads(8)
            split_heads(9)

            def copy_values(n):
                act.wait_ge(proj_done, n)
                nc.scalar.activation(v_sb[:, n - 10, :], work[:, BANK_OF[n], :], ACT.Copy).then_inc(proj_copied, 1)

            def exps(g):
                heads = GROUPS[g][1]
                act.wait_ge(max_ready, g + 1)
                if g == 2:
                    act.wait_ge(proj_done, 11)
                if g >= 4:
                    act.wait_ge(probs_turned, g - 1)
                w = 512 // len(heads)
                for n in range(len(heads)):
                    done = nc.scalar.activation(probs(g)[:, n * w:(n + 1) * w], work[:, S_BANKS[g % 2], n * w:(n + 1) * w],
                                                ACT.Exp, scale=SCALE, bias=amax[:, g, n:n + 1], accum_out=asum[:, g, n:n + 1])
                done.then_inc(exp_done, 1)

            def copy_output(qb):
                act.wait_ge(att_done, 2 if qb == 0 else len(GROUPS))
                nc.scalar.activation(att_y[:, :, qb * P:(qb + 1) * P], work[:, O_BANK, :].rearrange("p (k t) -> p k t", k=4),
                                     ACT.Copy).then_inc(att_copied, 1)

            act.wait_ge(centred, 1)
            nc.scalar.activation(ln_tmp, conv_y, ACT.Square).then_inc(squared, 1)
            act.wait_ge(var_ready, 1)
            nc.scalar.activation(ln_s[:, 1, :], ln_s[:, 0, :], ACT.Sqrt).then_inc(root_ready, 1)
            copy_values(10)
            act.wait_ge(normed, 1)
            for c in range(CB):
                done = nc.scalar.activation(ln_tmp[:, c, :], conv_y[:, c, :], ACT.Sigmoid,
                                            scale=cols[:, LN_G + c:LN_G + c + 1], bias=cols[:, LN_B + c:LN_B + c + 1])
            done.then_inc(swish_sig, 1)
            exps(0)
            exps(1)
            copy_values(11)
            exps(2)
            exps(3)
            copy_output(0)
            for g in range(4, len(GROUPS)):
                exps(g)

            def root_h(t):
                act.wait_ge(h_mean, 1 if t == 0 else 3)
                nc.scalar.activation(stat[:, 12 + t:13 + t], stat[:, 10 + t:11 + t], ACT.Sqrt).then_inc(h_root, 1)

            def square_h1(half):
                act.wait_ge(h1_copied, half + 1)
                at = T1_PARTS + half * HALF
                mean_square(hn[:, 1, half * HALF:(half + 1) * HALF], region_m[:, at:at + HALF], (stat[:, 9:10], stat[:, 0:1])[half],
                            h_squared)

            def cast_part(t, n):
                if n == 0:
                    act.wait_ge(h_scale, t + 1)
                    nc.scalar.activation(hn_parts[t][:, 0, :], hn[:, t, :], ACT.Copy, scale=stat[:, 14 + t:15 + t]).then_inc(part_act, 1)
                else:
                    act.wait_ge(part_dve, t + 1)
                    nc.scalar.activation(hn_parts[t][:, 1, :], hn[:, t, :], ACT.Copy).then_inc(part_act, 1)

            def copy_logits(t):
                act.wait_ge(logits_done, t + 1)
                nc.scalar.activation(logits_t[:, t * P:(t + 1) * P], work[0:E, LOGITS_BANKS[t], 0:P], ACT.Copy)\
                    .then_inc(logits_t_ready, 1)

            act.wait_ge(h_copied, 1)
            act.wait_ge(conv_ready, 1)
            mean_square(hn[:, 0, :], region_m[:, 1024:2048], stat[:, 8:9], h_squared)
            copy_output(1)
            act.wait_ge(moe_zeroed, 1)
            act.dma_start(bdown_sb[0:E, :], b_down).then_inc(bdown_in, 16)
            root_h(0)
            cast_part(0, 0)
            cast_part(0, 1)
            square_h1(0)
            square_h1(1)
            root_h(1)
            cast_part(1, 0)
            copy_logits(0)
            copy_logits(1)
            cast_part(1, 1)
            act.dma_start(final_gain, norm_final_g.partition_broadcast(P)).then_inc(final_gain_in, 16)
            act.wait_ge(top_diff, 1)
            nc.scalar.activation(top_w[:, 1, :, :], top_w[:, 0, :, :], ACT.Exp).then_inc(top_exp, 1)
            act.wait_ge(gates_turned, 1)
            act.wait_ge(moe_zeroed, 2)
            nc.scalar.activation(gates_t[0:E, :], work[0:E, TURN_BANK, 0:SEQ], ACT.Copy).then_inc(gates_t_ready, 1)

            def expert_pass(n, is_first=False):
                act.wait_ge(gate_clamped, n + 1)
                nc.scalar.activation(sig_h, gate_h, ACT.Sigmoid, scale=SWIGLU_ALPHA).then_inc(sig_ready, 1)
                act.wait_ge(act_turned, n + 1)
                nc.scalar.activation(act_t_flat, work[:, GATE_BANK, :], ACT.Copy).then_inc(act_t_ready, 1)
                act.wait_ge(weighted_turned, n + 1)
                if not is_first:
                    act.wait_ge(scattered, n * HALVES)
                nc.scalar.activation(scatter_flat, work[:, TURN_BANK, :], ACT.Copy).then_inc(scatter_ready, 1)

            def copy_results(n):
                act.wait_ge(slots_used, n * CHUNKS + CHUNKS)
                nc.scalar.activation(y_sb, work[:, OUT_BANK, :], ACT.Copy).then_inc(y_ready, 1)

            def expert(e, k, turn):
                if k > 0:
                    copy_results(e - 1)
                expert_pass(e, is_first=(k == 0))

            def extra(e, r, o):
                expert_pass(o + E)
                copy_results(o + E)

            experts(act, expert)
            total = experts_over(act)
            extras(act, extra, total)
            nc.scalar.activation(stat[:, 15:16], stat[:, 14:15], ACT.Sqrt).then_inc(o_root, 1)
            for t in range(TB):
                for h in range(2):
                    act.wait_ge(scattered, total * (HALVES * (SEQ // CAP - 1)) + (HALVES * (E - 1) + 2 * t + h + 1))
                    mean_square(resid[:, t, h * HALF:(h + 1) * HALF], work[:, GATE_BANK + h, :],
                                stat[:, 2 * t + h:2 * t + h + 1], o_squared)
                act.wait_ge(o_mean, 2 * t + 2)
                nc.scalar.activation(stat[:, 8 + t:9 + t], stat[:, 6 + t:7 + t], ACT.Sqrt).then_inc(o_root, 1)

        @block.vector
        def _(dve):
            V = nc.vector

            def inv_rms(n, src, mid, into, squared_sem, mean_sem, root_sem, scale_sem, roots_before=0):
                dve.wait_ge(squared_sem, n + 1)
                V.tensor_scalar(mid[0], src, 1.0 / D, RMS_EPS, ALU.mult, ALU.add).then_inc(mean_sem, 1)
                dve.wait_ge(root_sem, n + 1 + roots_before)
                V.reciprocal(into, mid[1]).then_inc(scale_sem, 1)
                dve.wait_ge(scale_sem, n + 1)

            def inv_rms_of_halves(n, squared_before, first, second, partial, mid, into, squared_sem, mean_sem, root_sem, scale_sem,
                                  roots_before=0):
                dve.wait_ge(squared_sem, squared_before + 1)
                V.tensor_scalar(partial, first, 1.0 / D, RMS_EPS, ALU.mult, ALU.add).then_inc(mean_sem, 1)
                dve.wait_ge(mean_sem, squared_before + 1)
                dve.wait_ge(squared_sem, squared_before + 2)
                V.tensor_scalar(mid[0], second, 1.0 / D, partial, ALU.mult, ALU.add).then_inc(mean_sem, 1)
                dve.wait_ge(root_sem, n + 1 + roots_before)
                V.reciprocal(into, mid[1]).then_inc(scale_sem, 1)
                dve.wait_ge(scale_sem, n + 1)

            for t in range(TB):
                inv_rms(t, stat[:, t:t + 1], (stat[:, 2 + t:3 + t], stat[:, 4 + t:5 + t]), stat[:, 6 + t:7 + t],
                        x_squared, x_mean, x_root, x_scale)
                V.tensor_scalar(xn[:, t, :], x_sb[:, t, :], stat[:, 6 + t:7 + t], None, ALU.mult).then_inc(xn_ready, 1)
            dve.wait_ge(cols_ready, 1)
            for n in range(4):
                t, g = n // 2, n % 2
                dve.wait_ge(xn_turned, n + 1)
                V.tensor_tensor(xn_t[:, 4 * g:4 * g + 4, t * P:(t + 1) * P], work[:, n, :].rearrange("p (k t) -> p k t", k=4),
                                cols[:, G_MIX + 4 * g:G_MIX + 4 * g + 4].unsqueeze(2).to_broadcast([P, 4, P]),
                                ALU.mult).then_inc(xnt_ready, 1)

            dve.wait_ge(proj_copied, 1)
            V.scalar_tensor_tensor(fg[:, 1, :], fg[:, 0, :], -1.0, fg[:, 0, :], ALU.mult, ALU.min).then_inc(fg_step, 1)
            dve.wait_ge(decay_exp, 1)
            V.tensor_scalar(fg[:, 3, :], fg[:, 2, :], 1.0, None, ALU.add).then_inc(fg_step, 1)
            dve.wait_ge(decay_exp, 2)
            V.scalar_tensor_tensor(fg[:, 5, :], fg[:, 0, :], 0.0, fg[:, 4, :], ALU.min, ALU.subtract).then_inc(fg_step, 1)
            V.memset(fg[:, 1, :], 1.0).then_inc(fg_step, 1)
            dve.wait_ge(fg_step, 4)
            V.tensor_tensor_scan(fg[:, 4, :], fg[:, 1, :], fg[:, 5, :], 0.0, ALU.mult, ALU.add).then_inc(fg_step, 1)
            dve.wait_ge(fg_step, 5)
            V.tensor_scalar(fg[:, 2, :], fg[:, 4, :], 1.0 / SCALE, None, ALU.mult).then_inc(decay_ready, 1)
            V.tensor_scalar(fg[:, 3, :], fg[:, 4, :], -1.0 / SCALE, None, ALU.mult).then_inc(decay_ready, 1)

            V.memset(channel_sum, 0.0).then_inc(sum_cleared, 1)
            dve.wait_ge(sum_cleared, 1)
            with dve.Fori(0, CB) as c:
                dve.wait_ge(taps_started, 2 * c + 2)
                for j in range(FIRST, TAPS):
                    acc = (conv_y if (j - FIRST) % 2 == 0 else conv_odd)[:, c, :]
                    if j >= FIRST + 2:
                        dve.wait_ge(tap_done, c * OPS + (j - FIRST - 1))
                    V.scalar_tensor_tensor(acc, u_pad[:, c, j:j + SEQ], dw_cols[:, c, j:j + 1], acc, ALU.mult, ALU.add)\
                        .then_inc(tap_done, 1)
                dve.wait_ge(tap_done, c * OPS + OPS - 3)
                V.tensor_tensor(conv_y[:, c, :], conv_y[:, c, :], conv_odd[:, c, :], ALU.add).then_inc(tap_done, 1)
                dve.wait_ge(tap_done, c * OPS + OPS - 2)
                dve.wait_ge(pool_taps, (c + 1) * POOL_STEPS)
                V.tensor_tensor(conv_y[:, c, :], conv_y[:, c, :], conv_pool[:, c, :], ALU.add).then_inc(tap_done, 1)
                dve.wait_ge(tap_done, c * OPS + OPS - 1)
                V.tensor_tensor(channel_sum, channel_sum, conv_y[:, c, :], ALU.add).then_inc(tap_done, 1)

            dve.wait_ge(mean_done, 1)
            V.tensor_tensor(conv_y, conv_y, work[:, MEAN_BANK, 0:SEQ].unsqueeze(1).to_broadcast([P, CB, SEQ]), ALU.subtract)\
                .then_inc(centred, 1)

            def row_max(g):
                heads = GROUPS[g][1]
                w = 512 // len(heads)
                dve.wait_ge(scores_done, g + 1)
                V.reduce_max(amax[:, g, 0:len(heads)], work[:, S_BANKS[g % 2], :].rearrange("p (n w) -> p n w", w=w),
                             AX.X).then_inc(max_step, 1)
                dve.wait_ge(max_step, g + 1)
                V.tensor_scalar(amax[:, g, 0:len(heads)], amax[:, g, 0:len(heads)], -SCALE, None, ALU.mult)\
                    .then_inc(max_ready, 1)

            def normalise(g):
                heads = GROUPS[g][1]
                w = 512 // len(heads)
                n = len(heads)
                dve.wait_ge(exp_done, g + 1)
                V.reciprocal(asum[:, g, 0:n], asum[:, g, 0:n]).then_inc(sum_step, 1)
                dve.wait_ge(sum_step, g + 1)
                view = probs(g).rearrange("p (n w) -> p n w", w=w)
                V.tensor_tensor(view, view, asum[:, g, 0:n].unsqueeze(2).to_broadcast([P, n, w]), ALU.mult)\
                    .then_inc(probs_ready, 1)

            def copy_turned(g):
                dve.wait_ge(probs_turned, g + 1)
                if g >= 2:
                    dve.wait_ge(att_done, g - 1)
                V.tensor_copy(probs_t[:, g % 2, :], work[:, T_BANK, :]).then_inc(probs_t_ready, 1)

            dve.wait_ge(squared, 1)
            V.tensor_reduce(channel_sum, ln_tmp.rearrange("p c t -> p t c"), AX.X, ALU.add).then_inc(squares_summed, 1)
            dve.wait_ge(var_done, 1)
            V.tensor_scalar(ln_s[:, 0, :], work[:, VAR_BANK, 0:SEQ], LN_EPS, None, ALU.add).then_inc(var_ready, 1)
            dve.wait_ge(root_ready, 1)
            V.reciprocal(ln_s[:, 0, :], ln_s[:, 1, :]).then_inc(ln_step, 1)
            dve.wait_ge(ln_step, 1)
            V.tensor_tensor(conv_y, conv_y, ln_s[:, 0, :].unsqueeze(1).to_broadcast([P, CB, SEQ]), ALU.mult)\
                .then_inc(normed, 1)
            row_max(0)
            row_max(1)
            dve.wait_ge(swish_sig, 1)
            for c in range(CB):
                V.tensor_scalar(conv_y[:, c, :], conv_y[:, c, :], cols[:, LN_G + c:LN_G + c + 1],
                                cols[:, LN_B + c:LN_B + c + 1], ALU.mult, ALU.add).then_inc(ln_step, 1)
            dve.wait_ge(ln_step, 1 + CB)
            V.tensor_tensor(conv_y, conv_y, ln_tmp, ALU.mult).then_inc(conv_ready, 1)
            normalise(0)
            normalise(1)
            row_max(2)
            copy_turned(0)
            copy_turned(1)
            for g in range(3, len(GROUPS) + 2):
                if g < len(GROUPS):
                    row_max(g)
                if g <= len(GROUPS):
                    normalise(g - 1)
                if g > 3:
                    copy_turned(g - 2)

            steps = [0]

            def then(ins):
                steps[0] += 1
                ins.then_inc(top_step, 1)
                dve.wait_ge(top_step, steps[0])

            dve.wait_ge(count_ready, 3)
            then(V.tensor_scalar(expert_no[:, :], count[:, 0:E], -1.0, None, ALU.add))
            dve.wait_ge(router_in, 32)

            def copy_h_turned(t, g):
                dve.wait_ge(h_turned, 2 * t + g + 1)
                V.tensor_tensor(h_t[:, 4 * g:4 * g + 4, t * P:(t + 1) * P], work[:, HT_BANKS[t][g], :].rearrange("p (k t) -> p k t", k=4),
                                cols[:, G_FFN + 4 * g:G_FFN + 4 * g + 4].unsqueeze(2).to_broadcast([P, 4, P]),
                                ALU.mult).then_inc(ht_ready, 1)

            def less_first_part(t):
                dve.wait_ge(part_act, 2 * t + 1)
                V.scalar_tensor_tensor(hn[:, t, :], hn[:, t, :], stat[:, 14 + t:15 + t], hn_parts[t][:, 0, :],
                                       ALU.mult, ALU.subtract).then_inc(part_dve, 1)

            def choose():
                for t in range(TB):
                    dve.wait_ge(logits_turned, t + 1)
                    V.scalar_tensor_tensor(logits[:, t, :], work[:, CHOICE_BANKS[t], 0:E], stat[:, 14 + t:15 + t], br_row[:, :],
                                           ALU.mult, ALU.add).then_inc(logits_scaled, 1)
                for t in range(TB):
                    dve.wait_ge(logits_scaled, t + 1)
                    V.max(out=top8[:, t, :], in_=logits[:, t, :]).then_inc(largest_ready, 1)
                for t in range(TB):
                    dve.wait_ge(largest_ready, t + 1)
                    done = V.max_index(out=top8_i[:, t, :], in_max=top8[:, t, :], in_values=logits[:, t, :])
                then(done)
                then(V.tensor_copy(top_i[:, :, :], top8_i[:, :, 0:TOP_K]))
                for t in range(TB):
                    V.tensor_tensor(onehot[:, 0, t, :, :], expert_no[:, :].unsqueeze(1).to_broadcast([P, TOP_K, E]),
                                    top_i[:, t, :].unsqueeze(2).to_broadcast([P, TOP_K, E]), ALU.is_equal).then_inc(onehot_ready, 1)
                for t in range(TB):
                    dve.wait_ge(onehot_ready, t + 1)
                    V.tensor_reduce(chosen[:, t, :], onehot[:, 0, t, :, :].rearrange("p k e -> p e k"), AX.X, ALU.add)\
                        .then_inc(choice_ready, 1)
                dve.wait_ge(choice_ready, TB)
                V.tensor_copy(chosen_b[:, :, :], chosen[:, :, :]).then_inc(chosen_ready, 1)

            dve.wait_ge(h_done, 1)
            dve.wait_ge(x_again_in, 16)
            V.tensor_tensor(hn[:, 0, :], resid[:, 0, :], x_again[:, 0, :], ALU.add).then_inc(h_copied, 1)
            copy_h_turned(0, 0)
            copy_h_turned(0, 1)
            inv_rms(0, stat[:, 8:9], (stat[:, 10:11], stat[:, 12:13]), stat[:, 14:15], h_squared, h_mean, h_root, h_scale)
            less_first_part(0)
            for half in (slice(0, HALF), slice(HALF, D)):
                dve.wait_ge(h_done, 2 + half.start // HALF)
                V.tensor_tensor(hn[:, 1, half], resid[:, 1, half], x_again[:, 1, half], ALU.add).then_inc(h1_copied, 1)
            copy_h_turned(1, 0)
            inv_rms_of_halves(1, 1, stat[:, 9:10], stat[:, 0:1], stat[:, 1:2], (stat[:, 11:12], stat[:, 13:14]), stat[:, 15:16],
                              h_squared, h_mean, h_root, h_scale)
            copy_h_turned(1, 1)
            less_first_part(1)
            choose()
            dve.wait_ge(places_done, 1)
            V.tensor_tensor(place[:, :, 0:E], work[:, TURN_BANK, 0:TB * E].rearrange("p (t e) -> p t e", t=TB), chosen[:, :, :],
                            ALU.mult).then_inc(place_ready, 1)
            dve.wait_ge(place_ready, 1)

            def select_tokens(e, r, g):
                dve.wait_ge(gathered, g)
                for t in range(TB):
                    done = V.tensor_scalar(select[:, t, :], count[:, bass.ds(r * CAP, CAP)], place[:, t, bass.ds(e, 1)], None,
                                           ALU.is_equal)
                done.then_inc(select_ready, 1)

            def weigh_tokens(e, r, n, is_first=False):
                if not is_first:
                    dve.wait_ge(weighted_turned, n)
                for t in range(TB):
                    done = V.tensor_scalar(weighted[:, t, CAP:2 * CAP], count[:, bass.ds(r * CAP, CAP)],
                                           place[:, t, bass.ds(e, 1)], gates[:, t, bass.ds(e, 1)], ALU.is_equal, ALU.mult)
                done.then_inc(weighted_ready, 1)

            def expert_pass(n):
                dve.wait_ge(slots_used, n * CHUNKS + UP_CHUNKS)
                V.tensor_scalar(gate_h, work[:, GATE_BANK, :], SWIGLU_LIMIT, None, ALU.min).then_inc(gate_clamped, 1)
                V.tensor_scalar(up_h, work[:, UP_BANK, :], SWIGLU_LIMIT, -SWIGLU_LIMIT, ALU.min, ALU.max).then_inc(up_clamped, 1)
                dve.wait_ge(gate_clamped, n + 1)
                dve.wait_ge(sig_ready, n + 1)
                V.tensor_tensor(sig_h, sig_h, gate_h, ALU.mult).then_inc(glu_ready, 1)
                dve.wait_ge(glu_ready, n + 1)
                dve.wait_ge(up_clamped, n + 1)
                V.scalar_tensor_tensor(up_h, up_h, 1.0, sig_h, ALU.add, ALU.mult).then_inc(act_ready, 1)

            def copy_tokens(g):
                dve.wait_ge(gathered, g + 1)
                V.tensor_tensor(tok_t, work[:, OUT_BANK, :].rearrange("p (k c) -> p k c", k=KB),
                                cols[:, G_FFN:G_FFN + KB].unsqueeze(2).to_broadcast([P, KB, CAP]), ALU.mult).then_inc(tok_t_ready, 1)

            select_tokens(0, 0, 0)
            V.tensor_tensor(top_w[:, 0, :, :], top8[:, :, 0:TOP_K], top8[:, :, 0:1].to_broadcast([P, TB, TOP_K]),
                            ALU.subtract).then_inc(top_diff, 1)
            copy_tokens(0)
            dve.wait_ge(top_exp, 1)
            then(V.reduce_sum(top_s[:, 0, :], top_w[:, 1, :, :], AX.X))
            then(V.reciprocal(top_s[:, 1, :], top_s[:, 0, :]))
            then(V.tensor_tensor(top_w[:, 2, :, :], top_w[:, 1, :, :], top_s[:, 1, :].unsqueeze(2).to_broadcast([P, TB, TOP_K]),
                                 ALU.mult))
            for t in range(TB):
                then(V.tensor_tensor(onehot[:, 1, t, :, :], onehot[:, 0, t, :, :],
                                     top_w[:, 2, t, :].unsqueeze(2).to_broadcast([P, TOP_K, E]), ALU.mult))
            V.tensor_reduce(gates[:, :, :], onehot[:, 1, :, :, :].rearrange("p t k e -> p t e k"), AX.X, ALU.add)\
                .then_inc(gates_ready, 1)
            dve.wait_ge(gates_ready, 1)
            then(V.tensor_scalar(over_f[:, 0, :], work[0:1, TURN_BANK, TB * E:TB * E + E], float(CAP), None, ALU.is_gt))
            then(V.memset(over_f[:, 3, :], 1.0))
            then(V.tensor_tensor_scan(over_f[:, 1, :], over_f[:, 3, :], over_f[:, 0, :], 0.0, ALU.mult, ALU.add))
            then(V.tensor_tensor(over_f[:, 2, :], over_f[:, 1, :], over_f[:, 0, :], ALU.subtract))
            then(V.tensor_copy(over[:, 0, :], over_f[:, 0, :]))
            then(V.tensor_copy(over[:, 1, :], over_f[:, 2, :]))
            V.tensor_copy(over_all[:, :], over_f[:, 1, E - 1:E]).then_inc(over_ready, 1)

            def expert(e, k, turn):
                weigh_tokens(e, 0, e, is_first=(k == 0))
                select_tokens(e + 1, 0, e + 1)
                expert_pass(e)
                copy_tokens(e + 1)

            experts(dve, expert)

            def extra(e, r, o):
                select_tokens(e, r, o + (E + 1))
                copy_tokens(o + (E + 1))
                weigh_tokens(e, r, o + E)
                expert_pass(o + E)

            dve.wait_ge(slots_used, E * CHUNKS)
            V.tensor_copy(y_sb, work[:, OUT_BANK, :]).then_inc(y_ready, 1)
            extras(dve, extra, experts_over(dve))
            dve.wait_ge(final_gain_in, 16)
            for t in range(TB):
                inv_rms_of_halves(t, 2 * t, stat[:, 2 * t:2 * t + 1], stat[:, 2 * t + 1:2 * t + 2], stat[:, 4 + t:5 + t],
                                  (stat[:, 6 + t:7 + t], stat[:, 8 + t:9 + t]), stat[:, 10 + t:11 + t],
                                  o_squared, o_mean, o_root, o_scale, roots_before=1)
                for h in range(2):
                    half = slice(h * HALF, (h + 1) * HALF)
                    V.scalar_tensor_tensor(result[:, t, half], resid[:, t, half], stat[:, 10 + t:11 + t], final_gain[:, half],
                                           ALU.mult, ALU.mult).then_inc(result_ready, 1)

        @block.tensor
        def _(pe):
            def mm(out_, lhsT, rhs, start, stop):
                return nc.tensor.matmul(out_, lhsT, rhs, start=start, stop=stop, skip_group_check=True)

            def keep_warm(n, out_):
                for _ in range(n):
                    mm(out_, ident[:, :], ident[:, :], True, True)

            pe.wait_ge(ident_ready, 1)
            keep_warm(10, resid[:, 0, 0:P])

            def turn_normed(n):
                t, g = n // 2, n % 2
                pe.wait_ge(xn_ready, t + 1)
                for j in range(4):
                    last = nc.tensor.transpose(work[:, n, j * P:(j + 1) * P], xn[:, t, (4 * g + j) * P:(4 * g + j + 1) * P], ident[:, :])
                last.then_inc(xn_turned, 1)

            turn_normed(0)
            turn_normed(1)
            pe.wait_ge(vecs_in, 16 * 6)
            nc.tensor.transpose(work[:, 3, 0:36], vec_rows, ident[0:36, 0:36])
            pe.wait_ge(dw_in, 16)
            for c in range(CB):
                last = nc.tensor.transpose(work[:, 3, 64 + 32 * c:64 + 32 * c + TAPS], dw_rows[:, c * P:(c + 1) * P],
                                           ident[0:TAPS, 0:TAPS])
            last.then_inc(vecs_turned, 1)
            turn_normed(2)
            pe.wait_ge(cols_ready, 2)
            turn_normed(3)

            def arrived(name):
                pe.wait_ge(slot_full[first_slot(name)], 16)

            def columns(bank, at, name, c):
                for kb in range(KB):
                    last = mm(work[:, bank, at:at + SEQ], piece(name)[:, kb, c * P:(c + 1) * P], xn_t[:, kb, :], kb == 0, kb == KB - 1)
                return last

            keep_warm(4, resid[:, 0, 0:P])
            pe.wait_ge(xnt_ready, 4)
            pe.wait_ge(wf_in, 16)
            for kb in range(KB):
                last = mm(work[0:HEADS, 0, 0:SEQ], wf_sb[:, kb, :], xn_t[:, kb, :], kb == 0, kb == KB - 1)
            last.then_inc(proj_done, 1)
            for c in range(CB):
                if c == 3:
                    pe.wait_ge(proj_copied, 1)
                for at, name in ((0, "glu_a"), (SEQ, "glu_g")):
                    if c % 2 == 0:
                        pe.wait_ge(slot_full[first_slot(name) + c // 2], 16)
                    last = columns(BANK_OF[2 + c], at, name, c)
                last.then_inc(proj_done, 1)
            for n in range(6, 10):
                name = "q" if n < 8 else "k"
                if n % 2 == 0:
                    arrived(name)
                pe.wait_ge(proj_copied, n - 4)
                columns(BANK_OF[n], 0, name, 2 * (n % 2))
                last = columns(BANK_OF[n], SEQ, name, 2 * (n % 2) + 1)
                last.then_inc(proj_done, 1)

            def channel_mean(bank):
                return mm(work[:, bank, 0:SEQ], mean_w[:, :], channel_sum, True, True)

            def values(n, blocks):
                for kb in blocks:
                    last = mm(work[:, BANK_OF[n], :], xn_t[:, kb, (n - 10) * P:(n - 9) * P], piece("v")[:, kb, :], kb == 0, kb == KB - 1)
                return last

            arrived("v")
            pe.wait_ge(proj_copied, 6)
            values(10, range(0, 3))
            pe.wait_ge(consts_ready, 5)
            pe.wait_ge(tap_done, CB * OPS)
            pe.wait_ge(proj_copied, 7)
            channel_mean(MEAN_BANK).then_inc(mean_done, 1)
            values(10, range(3, KB)).then_inc(proj_done, 1)

            def scores(g):
                qb, heads = GROUPS[g]
                bank, w = S_BANKS[g % 2], 512 // len(heads)
                if g >= 2:
                    pe.wait_ge(exp_done, g - 1)
                keys = (qb + 1) * P
                for n, h in enumerate(heads):
                    mm(work[:, bank, n * w:n * w + keys], q_aug[:, h, qb * P:(qb + 1) * P], k_aug[:, h, 0:keys], True, False)
                    last = mm(work[:, bank, n * w + qb * P:n * w + keys], ident_b[:, :], causal[:, :], False, True)
                last.then_inc(scores_done, 1)

            def turn(g):
                pe.wait_ge(probs_ready, g + 1)
                if g >= 1:
                    pe.wait_ge(probs_t_ready, g)
                else:
                    pe.wait_ge(proj_copied, 11)
                for b in range(4):
                    last = nc.tensor.transpose(work[:, T_BANK, b * P:(b + 1) * P], probs(g)[:, b * P:(b + 1) * P], ident[:, :])
                last.then_inc(probs_turned, 1)

            def weigh_values(g):
                qb, heads = GROUPS[g]
                pe.wait_ge(probs_t_ready, g + 1)
                if g == 2:
                    pe.wait_ge(att_copied, 1)
                b = 0
                for h in heads:
                    to = work[DH * (h % 2):DH * (h % 2) + DH, O_BANK, (h // 2) * P:(h // 2 + 1) * P]
                    for s in range(qb + 1):
                        last = mm(to, v_sb[:, s, h * DH:(h + 1) * DH], probs_t[:, g % 2, b * P:(b + 1) * P], s == 0, s == qb)
                        b += 1
                last.then_inc(att_done, 1)

            def project(name, t, h, blocks=range(4)):
                for kb in blocks:
                    last = mm(resid[:, t, h * HALF:(h + 1) * HALF],
                              (conv_y if name == "out_conv" else att_y)[:, kb, t * P:(t + 1) * P],
                              piece(name)[:, kb, h * HALF:(h + 1) * HALF], name == "out_conv" and kb == 0, False)
                return last

            pe.wait_ge(squares_summed, 1)
            pe.wait_ge(proj_copied, 9)
            channel_mean(VAR_BANK).then_inc(var_done, 1)
            pe.wait_ge(decay_in, 32)
            pe.wait_ge(centred, 1)
            scores(0)
            pe.wait_ge(proj_copied, 10)
            scores(1)
            values(11, range(KB)).then_inc(proj_done, 1)
            scores(2)
            turn(0)
            pe.wait_ge(conv_ready, 1)
            arrived("out_conv")
            project("out_conv", 0, 0, range(0, 2))
            weigh_values(0)
            turn(1)
            scores(3)
            weigh_values(1)
            fill = [("out_conv", 0, 1), ("out_att", 0, 0), ("out_att", 0, 1), ("out_conv", 1, 0), ("out_conv", 1, 1)]
            arrived("out_att")

            def fill_in(count_):
                for _ in range(count_):
                    name, t, h = fill.pop(0)
                    if (name, t, h) == ("out_att", 0, 0):
                        pe.wait_ge(att_copied, 1)
                    last = project(name, t, h)
                    if (name, t, h) == ("out_att", 0, 1):
                        last.then_inc(h_done, 1)
                    if (name, t, h) == ("out_conv", 1, 1):
                        last.then_inc(conv_added, 1)

            project("out_conv", 0, 0, range(2, 4))
            turn(2)
            scores(4)
            fill_in(1)
            weigh_values(2)
            turn(3)
            scores(5)
            fill_in(1)
            weigh_values(3)
            turn(4)
            fill_in(1)
            weigh_values(4)
            turn(5)
            fill_in(1)
            weigh_values(5)

            def turn_h(t, g):
                if t == 0:
                    pe.wait_ge(h_copied, 1)
                    pe.wait_ge(exp_done, len(GROUPS))
                else:
                    pe.wait_ge(h1_copied, g + 1)
                    if g > 0:
                        pe.wait_ge(ht_ready, 1)
                for j in range(4):
                    last = nc.tensor.transpose(work[:, HT_BANKS[t][g], j * P:(j + 1) * P], hn[:, t, (4 * g + j) * P:(4 * g + j + 1) * P],
                                               ident[:, :])
                last.then_inc(h_turned, 1)

            def route(t, blocks):
                for kb in blocks:
                    last = mm(work[0:E, LOGITS_BANKS[t], 0:P], wr_sb[:, kb, :], h_t[:, kb, t * P:(t + 1) * P],
                              kb == 0, kb == KB - 1)
                return last

            def turn_logits(t):
                pe.wait_ge(logits_t_ready, t + 1)
                nc.tensor.transpose(work[:, CHOICE_BANKS[t], 0:E], logits_t[:, t * P:(t + 1) * P], ident[0:E, 0:E])\
                    .then_inc(logits_turned, 1)

            def add_x(t, h):
                return mm(resid[:, t, h * HALF:(h + 1) * HALF], ident[:, :], x_again[:, t, h * HALF:(h + 1) * HALF], False, False)

            turn_h(0, 0)
            turn_h(0, 1)
            fill_in(1)
            pe.wait_ge(att_copied, 2)
            project("out_att", 1, 0).then_inc(h_done, 1)
            project("out_att", 1, 1).then_inc(h_done, 1)
            turn_h(1, 0)
            pe.wait_ge(router_in, 32)
            pe.wait_ge(ht_ready, 2)
            pe.wait_ge(probs_t_ready, len(GROUPS))
            route(0, range(0, KB // 2))
            turn_h(1, 1)
            route(0, range(KB // 2, KB)).then_inc(logits_done, 1)
            pe.wait_ge(ht_ready, 3)
            route(1, range(0, KB // 2))
            turn_logits(0)
            pe.wait_ge(ht_ready, 4)
            route(1, range(KB // 2, KB)).then_inc(logits_done, 1)
            turn_logits(1)
            for t, h in ((0, 0), (0, 1), (1, 0)):
                add_x(t, h)
            pe.wait_ge(chosen_ready, 1)
            for t in range(TB):
                for s in range(t + 1):
                    mm(work[:, TURN_BANK, t * E:(t + 1) * E], (upto if s == t else ones_b)[:, :], chosen_b[:, s, :], s == 0, s == t)
            for s in range(TB):
                last = mm(work[0:1, TURN_BANK, TB * E:TB * E + E], ones_b[:, 0:1], chosen_b[:, s, :], s == 0, s == TB - 1)
            last.then_inc(places_done, 1)
            add_x(1, 1).then_inc(x_added, 1)

            def gather(g):
                pe.wait_ge(select_ready, g + 1)
                for kb in range(KB):
                    for n in range(3 * TB):
                        last = mm(work[:, OUT_BANK, kb * CAP:(kb + 1) * CAP], hn_parts[n // 3][:, n % 3, kb * P:(kb + 1) * P],
                                  select[:, n // 3, :], n == 0, n == 3 * TB - 1)
                last.then_inc(gathered, 1)

            def turn_gates():
                pe.wait_ge(gates_ready, 1)
                pe.wait_ge(over_ready, 1)
                for t in range(TB):
                    last = nc.tensor.transpose(work[0:E, TURN_BANK, t * P:(t + 1) * P], gates[:, t, :], ident[:, :])
                last.then_inc(gates_turned, 1)

            def add_bdown():
                pe.wait_ge(bdown_in, 16)
                pe.wait_ge(gates_t_ready, 1)
                for t in range(TB):
                    for h in range(2):
                        mm(resid[:, t, h * HALF:(h + 1) * HALF], gates_t[:, t * P:(t + 1) * P], bdown_sb[:, h * HALF:(h + 1) * HALF], False, False)

            def scatter(n, t):
                if t == 0:
                    pe.wait_ge(scatter_ready, n + 1)
                    pe.wait_ge(y_ready, n + 1)
                for h in range(2):
                    mm(resid[:, t, h * HALF:(h + 1) * HALF], scatter_sb[:, h * TB + t, :], y_sb, False, False).then_inc(scattered, 1)

            def slot_arrived(k, i, turn):
                pe.wait_ge(slot_full[slot_of(k, i)], turn * (16 * ROUNDS) + 16 * uses_of(k, i))

            def expert_pass(e, n, g, next_g, arrived_chunk, slot, is_first=False):
                for bank in (GATE_BANK, UP_BANK):
                    mm(work[:, bank, :], bias_sel[:, e // 2, :], bgu_parts[:, e % 2, bank * 512:(bank + 1) * 512], True, False)
                pe.wait_ge(tok_t_ready, g + 1)
                for kb in range(KB):
                    if is_first and kb == KB // 2:
                        turn_gates()
                    arrived_chunk(kb)
                    w = chunk(slot(kb))
                    for bank in (GATE_BANK, UP_BANK):
                        for h in range(2):
                            c = bank * D_FF + h * HALF
                            last = mm(work[CAP * h:CAP * (h + 1), bank, :], tok_t[:, kb, :], w[:, c:c + HALF], False, kb == KB - 1)
                    last.then_inc(slots_used, 1)
                    if kb == 0 and next_g is not None and not is_first:
                        scatter(n - 1, 0)
                    if kb == KB - 2:
                        if is_first:
                            pe.wait_ge(gates_t_ready, 1)
                        else:
                            pe.wait_ge(scatter_ready, n)
                        pe.wait_ge(weighted_ready, n + 1)
                        for h in range(2):
                            for t in range(TB):
                                last = nc.tensor.transpose(work[:, TURN_BANK, (h * TB + t) * P:(h * TB + t + 1) * P],
                                                           weighted[:, t, (1 - h) * CAP:(1 - h) * CAP + P], ident[:, :])
                        last.then_inc(weighted_turned, 1)
                if next_g is not None:
                    if not is_first:
                        pe.wait_ge(y_ready, n)
                    gather(next_g)
                if is_first:
                    add_bdown()
                elif next_g is not None:
                    scatter(n - 1, 1)
                pe.wait_ge(act_ready, n + 1)
                for j in range(4):
                    last = nc.tensor.transpose(work[:, GATE_BANK, j * P:(j + 1) * P], up_h[:, j * P:(j + 1) * P], ident[:, :])
                last.then_inc(act_turned, 1)
                pe.wait_ge(act_t_ready, n + 1)
                if next_g is not None:
                    pe.wait_ge(tok_t_ready, next_g + 1)
                for m in range(DOWN_CHUNKS):
                    arrived_chunk(UP_CHUNKS + m)
                    w = chunk(slot(UP_CHUNKS + m))
                    for b in range(2):
                        f = 2 * m + b
                        lhsT = act_t[:, f % 4, (f // 4) * CAP:(f // 4 + 1) * CAP]
                        for h in range(2):
                            last = mm(work[CAP * h:CAP * (h + 1), OUT_BANK, :], lhsT, w[:, b * D + h * HALF:b * D + (h + 1) * HALF],
                                      f == 0, f == FB - 1)
                    last.then_inc(slots_used, 1)

            pe.wait_ge(part_pool, TB)
            gather(0)
            pe.wait_ge(bias_sel_ready, 3)
            pe.wait_ge(bgu_cast, 4)
            experts(pe, lambda e, k, turn: expert_pass(e, e, e, e + 1, lambda i: slot_arrived(k, i, turn), lambda i: slot_of(k, i),
                                                       is_first=(k == 0)))
            for t in range(TB):
                scatter(E - 1, t)

            def extra(e, r, o):
                gather(o + (E + 1))
                expert_pass(e, o + E, o + (E + 1), None,
                            lambda i: pe.wait_ge(slot_full[slot_of(E, i)], o * 16 + 16 * uses_of(E, i)), lambda i: slot_of(E, i))
                for t in range(TB):
                    scatter(o + E, t)

            extras(pe, extra, experts_over(pe))


_INS = ["x", "norm_mix_g", "w_in", "b_f", "b_glu", "w_dw", "b_dw", "ln_g", "ln_b", "w_out", "norm_ffn_g",
        "w_router", "b_router", "w_gu", "b_gu", "w_down", "b_down", "norm_final_g"]


def kernel(**inputs):
    import concourse.bacc as bacc
    from concourse.bass_utils import run_bass_kernel_spmd

    nc = bacc.Bacc("TRN2", target_bir_lowering=False, num_devices=1, dynamic_dma_scratch_size=1024)
    arrays, args = {}, []
    for name in _INS:
        a = np.ascontiguousarray(inputs[name])
        arrays[f"in_{name}"] = a
        args.append(nc.dram_tensor(f"in_{name}", a.shape, mybir.dt.from_np(a.dtype), kind="ExternalInput").ap())
    result = nc.dram_tensor("result", inputs["x"].shape, F32, kind="ExternalOutput").ap()
    hybrid_layer(nc, *args, result)
    return run_bass_kernel_spmd(nc, [arrays], core_ids=[0]).results[0]["result"]
```
